# Optimizing a Trainium2 kernel written in Bass

```python
import numpy as np
import jax
import jax.numpy as jnp
from jax import lax

D_MODEL = 1024
BATCH = 1
SEQ = 256
DEPTH = 1

HEAD_DIM = 64
Q_BLOCK = 128
ROPE_THETA = 10000.0
RMS_EPS = 1e-5
NEG_INF = -1e30
FORCE_SCORE = 1e4
NSA_HEADS = 8
NSA_GROUPS = 2
NSA_REP = NSA_HEADS // NSA_GROUPS
NSA_BRANCHES = 3
CMP_LEN = 32
CMP_STRIDE = 16
SEL_BLOCK = 64
SEL_TOPK = 16
WINDOW = 512
FOX_HEADS = 8
MEM_HEADS = 4
MEM_HEAD_DIM = 128
MEM_LEN = 256
N_MIXERS = 3
N_EXPERTS = 32
TOP_K = 4
D_EXPERT = D_MODEL
SWIGLU_LIMIT = 7.0
SWIGLU_ALPHA = 1.702
MOE_BLOCK = 128

NSA_Q_W = NSA_HEADS * HEAD_DIM
NSA_KV_W = NSA_GROUPS * HEAD_DIM
FOX_W = FOX_HEADS * HEAD_DIM
MEM_W = MEM_HEADS * MEM_HEAD_DIM
IN_SPLITS = (
    NSA_Q_W,
    NSA_KV_W, NSA_KV_W,
    NSA_KV_W, NSA_KV_W,
    NSA_KV_W, NSA_KV_W,
    NSA_BRANCHES * NSA_HEADS,
    FOX_W, FOX_W, FOX_W,
    FOX_HEADS,
    MEM_W,
    N_MIXERS * D_MODEL,
)
D_IN = sum(IN_SPLITS)
IN_OFFSETS = tuple(int(o) for o in np.cumsum(IN_SPLITS)[:-1])

kernel_name = 'hybrid_nsa_fox_memory_moe_block'

def rms_norm(x, g):
    x32 = x.astype(jnp.float32)
    y = x32 * lax.rsqrt(jnp.mean(x32 * x32, axis=-1, keepdims=True) + RMS_EPS)
    return (y * g.astype(jnp.float32)).astype(x.dtype)

def rope_tables(seq, dim, dtype):
    inv = ROPE_THETA ** (-jnp.arange(0, dim, 2, dtype=jnp.float32) / dim)
    ang = jnp.arange(seq, dtype=jnp.float32)[:, None] * inv[None, :]
    return jnp.cos(ang).astype(dtype), jnp.sin(ang).astype(dtype)

def apply_rope(x, cos, sin):
    x1, x2 = jnp.split(x, 2, axis=-1)
    c = cos[:, None, :]
    s = sin[:, None, :]
    return jnp.concatenate([x1 * c - x2 * s, x2 * c + x1 * s], axis=-1)

def masked_softmax(s, mask):
    s = jnp.where(mask, s.astype(jnp.float32), NEG_INF)
    m = jnp.max(s, axis=-1, keepdims=True)
    e = jnp.where(mask, jnp.exp(s - m), 0.0)
    return e / jnp.maximum(jnp.sum(e, axis=-1, keepdims=True), 1e-30)

def compress_blocks(kv, pe, w1, w2):
    b, s, g, d = kv.shape
    kb = kv.reshape(b, s // CMP_STRIDE, CMP_STRIDE, g, d)
    blocks = jnp.concatenate([kb[:, :-1], kb[:, 1:]], axis=2)
    z = jnp.einsum('bnlgd,lde->bnge', blocks + pe[:, None, :], w1)
    return jax.nn.silu(z) @ w2

def nsa_mixer(q, kc, vc, ks, vs, kw, vw, gate_logits, pe_k, w1_k, w2_k, pe_v, w1_v, w2_v):
    b, s, h, d = q.shape
    scale = d ** -0.5
    nq = s // Q_BLOCK
    qg = q.reshape(b, s, NSA_GROUPS, NSA_REP, d)
    tpos = jnp.arange(s)

    kcmp = compress_blocks(kc, pe_k, w1_k, w2_k)
    vcmp = compress_blocks(vc, pe_v, w1_v, w2_v)
    n_cmp = kcmp.shape[1]
    cstart = jnp.arange(n_cmp) * CMP_STRIDE
    cmask = (cstart + CMP_LEN - 1)[None, :] <= tpos[:, None]
    s_c = jnp.einsum('bsgrd,bngd->bgrsn', qg, kcmp).astype(jnp.float32) * scale
    p_c = masked_softmax(s_c, cmask)
    o_cmp = jnp.einsum('bgrsn,bngd->bsgrd', p_c.astype(vcmp.dtype), vcmp)

    n_sel_blk = s // SEL_BLOCK
    n_top = min(SEL_TOPK, n_sel_blk)
    blk = jnp.arange(n_sel_blk)
    overlap = ((cstart[:, None] < (blk[None, :] + 1) * SEL_BLOCK)
               & (cstart[:, None] + CMP_LEN > blk[None, :] * SEL_BLOCK)).astype(jnp.float32)
    imp = jnp.einsum('bgrsn,nj->bgsj', p_c, overlap)
    cur = (tpos // SEL_BLOCK)[:, None]
    forced = (blk[None, :] == 0) | (blk[None, :] == cur) | (blk[None, :] == cur - 1)
    future = blk[None, :] * SEL_BLOCK > tpos[:, None]
    imp = jnp.where(forced, FORCE_SCORE, jnp.where(future, -FORCE_SCORE, imp))
    _, sel = lax.top_k(imp, n_top)

    kblk = ks.reshape(b, n_sel_blk, SEL_BLOCK, NSA_GROUPS, d).transpose(0, 3, 1, 2, 4)
    vblk = vs.reshape(b, n_sel_blk, SEL_BLOCK, NSA_GROUPS, d).transpose(0, 3, 1, 2, 4)
    bi = jnp.arange(b)[:, None, None, None]
    gi = jnp.arange(NSA_GROUPS)[None, :, None, None]
    offs = jnp.arange(SEL_BLOCK)
    n_keys = n_top * SEL_BLOCK
    q_chunks = qg.reshape(b, nq, Q_BLOCK, NSA_GROUPS, NSA_REP, d).transpose(1, 0, 2, 3, 4, 5)
    sel_chunks = sel.reshape(b, NSA_GROUPS, nq, Q_BLOCK, n_top).transpose(2, 0, 1, 3, 4)

    def sel_chunk(args):
        qi, si, ci = args
        kk = kblk[bi, gi, si].reshape(b, NSA_GROUPS, Q_BLOCK, n_keys, d)
        vv = vblk[bi, gi, si].reshape(b, NSA_GROUPS, Q_BLOCK, n_keys, d)
        kpos = (si[..., None] * SEL_BLOCK + offs).reshape(b, NSA_GROUPS, Q_BLOCK, n_keys)
        qpos = ci * Q_BLOCK + jnp.arange(Q_BLOCK)
        mask = (kpos <= qpos[None, None, :, None])[:, :, None]
        sc = jnp.einsum('btgrd,bgtkd->bgrtk', qi, kk).astype(jnp.float32) * scale
        p = masked_softmax(sc, mask)
        return jnp.einsum('bgrtk,bgtkd->btgrd', p.astype(vv.dtype), vv)

    o_slc = lax.map(sel_chunk, (q_chunks, sel_chunks, jnp.arange(nq)))
    o_slc = o_slc.transpose(1, 0, 2, 3, 4, 5).reshape(b, s, NSA_GROUPS, NSA_REP, d)

    n_prev = WINDOW // Q_BLOCK
    pad = ((0, 0), (WINDOW, 0), (0, 0), (0, 0))
    kwb = jnp.pad(kw, pad).reshape(b, nq + n_prev, Q_BLOCK, NSA_GROUPS, d)
    vwb = jnp.pad(vw, pad).reshape(b, nq + n_prev, Q_BLOCK, NSA_GROUPS, d)
    kband = jnp.concatenate([kwb[:, i:i + nq] for i in range(n_prev + 1)], axis=2)
    vband = jnp.concatenate([vwb[:, i:i + nq] for i in range(n_prev + 1)], axis=2)
    qb = qg.reshape(b, nq, Q_BLOCK, NSA_GROUPS, NSA_REP, d)
    qpos = jnp.arange(nq)[:, None] * Q_BLOCK + jnp.arange(Q_BLOCK)[None, :]
    kpos = jnp.arange(nq)[:, None] * Q_BLOCK - WINDOW + jnp.arange((n_prev + 1) * Q_BLOCK)[None, :]
    diff = qpos[:, :, None] - kpos[:, None, :]
    wmask = (diff >= 0) & (diff < WINDOW) & (kpos[:, None, :] >= 0)
    sw = jnp.einsum('bctgrd,bckgd->bcgrtk', qb, kband).astype(jnp.float32) * scale
    pw = masked_softmax(sw, wmask[None, :, None, None])
    o_win = jnp.einsum('bcgrtk,bckgd->bctgrd', pw.astype(vband.dtype), vband)
    o_win = o_win.reshape(b, s, NSA_GROUPS, NSA_REP, d)

    g = jax.nn.sigmoid(gate_logits.astype(jnp.float32)).astype(q.dtype)
    g = g.reshape(b, s, NSA_GROUPS, NSA_REP, NSA_BRANCHES)
    o = g[..., 0:1] * o_cmp + g[..., 1:2] * o_slc + g[..., 2:3] * o_win
    return o.reshape(b, s, h * d)

def fox_mixer(q, k, v, f_logits, b_forget):
    b, s, h, d = q.shape
    scale = d ** -0.5
    nq = s // Q_BLOCK
    logf = jax.nn.log_sigmoid(f_logits.astype(jnp.float32) + b_forget.astype(jnp.float32))
    cum = jnp.cumsum(logf, axis=1).transpose(0, 2, 1)
    q_chunks = q.reshape(b, nq, Q_BLOCK, h, d).transpose(1, 0, 2, 3, 4)
    c_chunks = cum.reshape(b, h, nq, Q_BLOCK).transpose(2, 0, 1, 3)
    kpos = jnp.arange(s)

    def block(args):
        qi, ci, idx = args
        sc = (jnp.einsum('bthd,bshd->bhts', qi, k).astype(jnp.float32) * scale
              + ci[..., None] - cum[:, :, None, :])
        qpos = idx * Q_BLOCK + jnp.arange(Q_BLOCK)
        p = masked_softmax(sc, kpos[None, :] <= qpos[:, None])
        return jnp.einsum('bhts,bshd->bthd', p.astype(v.dtype), v)

    o = lax.map(block, (q_chunks, c_chunks, jnp.arange(nq)))
    return o.transpose(1, 0, 2, 3, 4).reshape(b, s, h * d)

def memory_mixer(q, mem_h, w_mem_kv):
    b, s, h, d = q.shape
    m = mem_h.shape[1]
    k, v = jnp.split(mem_h @ w_mem_kv, 2, axis=-1)
    k = k.reshape(b, m, h, d)
    v = v.reshape(b, m, h, d)
    sc = jnp.einsum('bshd,bmhd->bhsm', q, k).astype(jnp.float32) * (d ** -0.5)
    p = jax.nn.softmax(sc, axis=-1)
    o = jnp.einsum('bhsm,bmhd->bshd', p.astype(v.dtype), v)
    return o.reshape(b, s, h * d)

def moe_ffn(h, w_router, b_router, w_gate_up, b_gate_up, w_down, b_down):
    b, s, d = h.shape
    t = b * s
    hf = h.reshape(t, d)
    logits = (hf @ w_router + b_router).astype(jnp.float32)
    top_val, top_idx = lax.top_k(logits, TOP_K)
    gate = jax.nn.softmax(top_val, axis=-1)
    n_assign = t * TOP_K
    e_flat = top_idx.reshape(n_assign)
    tok_flat = jnp.repeat(jnp.arange(t, dtype=jnp.int32), TOP_K)
    g_flat = gate.reshape(n_assign)
    order = jnp.argsort(e_flat, stable=True)
    e_sorted = e_flat[order]
    counts = jnp.bincount(e_flat, length=N_EXPERTS)
    starts = jnp.cumsum(counts) - counts
    padded = (counts + MOE_BLOCK - 1) // MOE_BLOCK * MOE_BLOCK
    pad_ends = jnp.cumsum(padded)
    pad_starts = pad_ends - padded
    dest = pad_starts[e_sorted] + jnp.arange(n_assign) - starts[e_sorted]
    n_blocks = -(-(n_assign + N_EXPERTS * (MOE_BLOCK - 1)) // MOE_BLOCK)
    n_slots = n_blocks * MOE_BLOCK
    slot_tok = jnp.full((n_slots,), t, jnp.int32).at[dest].set(tok_flat[order])
    slot_gate = jnp.zeros((n_slots,), jnp.float32).at[dest].set(g_flat[order])
    block_exp = jnp.minimum(
        jnp.searchsorted(pad_ends, jnp.arange(n_blocks) * MOE_BLOCK, side='right'), N_EXPERTS - 1)
    h_pad = jnp.concatenate([hf, jnp.zeros((1, d), hf.dtype)], axis=0)

    def expert_block(args):
        e, toks = args
        xt = h_pad[toks]
        gu = xt @ w_gate_up[e] + b_gate_up[e]
        g = jnp.minimum(gu[:, 0::2], SWIGLU_LIMIT)
        u = jnp.clip(gu[:, 1::2], -SWIGLU_LIMIT, SWIGLU_LIMIT)
        act = (u + 1.0) * g * jax.nn.sigmoid(SWIGLU_ALPHA * g)
        return act @ w_down[e] + b_down[e]

    out = lax.map(expert_block, (block_exp, slot_tok.reshape(n_blocks, MOE_BLOCK)))
    out = out.reshape(n_slots, d) * slot_gate[:, None].astype(out.dtype)
    y = jax.ops.segment_sum(out, slot_tok, num_segments=t + 1)[:t]
    return y.reshape(b, s, d)

def setup_inputs(seed: int = 0) -> dict:
    key = jax.random.key(seed)
    ks = jax.random.split(key, 32)
    L = DEPTH
    F = D_EXPERT

    def nrm(k, shape, scale):
        return jax.random.normal(k, shape, jnp.float32) * scale

    def gain(k, shape):
        return 1.0 + 0.02 * jax.random.normal(k, shape, jnp.float32)

    return {
        'x': nrm(ks[0], (BATCH, SEQ, D_MODEL), 1.0),
        'mem': nrm(ks[1], (BATCH, MEM_LEN, D_MODEL), 1.0),
        'g_mix': gain(ks[2], (L, D_MODEL)),
        'w_in': nrm(ks[3], (L, D_MODEL, D_IN), D_MODEL ** -0.5),
        'b_forget': jax.random.uniform(ks[4], (L, FOX_HEADS), jnp.float32, 1.0, 6.0),
        'b_merge': nrm(ks[5], (L, N_MIXERS * D_MODEL), 0.02),
        'nsa_pe_k': nrm(ks[6], (L, CMP_LEN, HEAD_DIM), 0.02),
        'nsa_w1_k': nrm(ks[7], (L, CMP_LEN, HEAD_DIM, HEAD_DIM), (CMP_LEN * HEAD_DIM) ** -0.5),
        'nsa_w2_k': nrm(ks[8], (L, HEAD_DIM, HEAD_DIM), HEAD_DIM ** -0.5),
        'nsa_pe_v': nrm(ks[9], (L, CMP_LEN, HEAD_DIM), 0.02),
        'nsa_w1_v': nrm(ks[10], (L, CMP_LEN, HEAD_DIM, HEAD_DIM), (CMP_LEN * HEAD_DIM) ** -0.5),
        'nsa_w2_v': nrm(ks[11], (L, HEAD_DIM, HEAD_DIM), HEAD_DIM ** -0.5),
        'g_mem': gain(ks[12], (L, D_MODEL)),
        'w_mem_kv': nrm(ks[13], (L, D_MODEL, 2 * MEM_W), D_MODEL ** -0.5),
        'w_branch_nsa': nrm(ks[14], (L, NSA_Q_W, D_MODEL), NSA_Q_W ** -0.5),
        'w_branch_fox': nrm(ks[15], (L, FOX_W, D_MODEL), FOX_W ** -0.5),
        'w_branch_mem': nrm(ks[16], (L, MEM_W, D_MODEL), MEM_W ** -0.5),
        'w_out': nrm(ks[17], (L, D_MODEL, D_MODEL), D_MODEL ** -0.5),
        'g_ffn': gain(ks[18], (L, D_MODEL)),
        'w_router': nrm(ks[19], (L, D_MODEL, N_EXPERTS), D_MODEL ** -0.5),
        'b_router': nrm(ks[20], (L, N_EXPERTS), 0.01),
        'w_gate_up': nrm(ks[21], (L, N_EXPERTS, D_MODEL, 2 * F), D_MODEL ** -0.5),
        'b_gate_up': nrm(ks[22], (L, N_EXPERTS, 2 * F), 0.02),
        'w_down': nrm(ks[23], (L, N_EXPERTS, F, D_MODEL), F ** -0.5),
        'b_down': nrm(ks[24], (L, N_EXPERTS, D_MODEL), 0.02),
        'g_final': gain(ks[25], (D_MODEL,)),
    }

def reference(x, mem, g_mix, w_in, b_forget, b_merge, nsa_pe_k, nsa_w1_k, nsa_w2_k, nsa_pe_v,
              nsa_w1_v, nsa_w2_v, g_mem, w_mem_kv, w_branch_nsa, w_branch_fox, w_branch_mem, w_out,
              g_ffn, w_router, b_router, w_gate_up, b_gate_up, w_down, b_down, g_final):
    b, s, _ = x.shape
    cos, sin = rope_tables(s, HEAD_DIM, x.dtype)

    def heads(t, n, d):
        return t.reshape(b, s, n, d)

    for l in range(DEPTH):
        h = rms_norm(x, g_mix[l])
        parts = jnp.split(h @ w_in[l], IN_OFFSETS, axis=-1)
        (q_a, k_c, v_c, k_s, v_s, k_w, v_w, nsa_gl,
         q_f, k_f, v_f, f_l, q_m, merge_l) = parts

        o_nsa = nsa_mixer(
            apply_rope(heads(q_a, NSA_HEADS, HEAD_DIM), cos, sin),
            apply_rope(heads(k_c, NSA_GROUPS, HEAD_DIM), cos, sin), heads(v_c, NSA_GROUPS, HEAD_DIM),
            apply_rope(heads(k_s, NSA_GROUPS, HEAD_DIM), cos, sin), heads(v_s, NSA_GROUPS, HEAD_DIM),
            apply_rope(heads(k_w, NSA_GROUPS, HEAD_DIM), cos, sin), heads(v_w, NSA_GROUPS, HEAD_DIM),
            nsa_gl, nsa_pe_k[l], nsa_w1_k[l], nsa_w2_k[l], nsa_pe_v[l], nsa_w1_v[l], nsa_w2_v[l])
        o_fox = fox_mixer(heads(q_f, FOX_HEADS, HEAD_DIM), heads(k_f, FOX_HEADS, HEAD_DIM),
                          heads(v_f, FOX_HEADS, HEAD_DIM), f_l, b_forget[l])
        o_mem = memory_mixer(heads(q_m, MEM_HEADS, MEM_HEAD_DIM), rms_norm(mem, g_mem[l]), w_mem_kv[l])

        gates = jax.nn.sigmoid((merge_l + b_merge[l]).astype(jnp.float32)).astype(x.dtype)
        g_nsa, g_fox, g_mem_br = jnp.split(gates, N_MIXERS, axis=-1)
        merged = (g_nsa * (o_nsa @ w_branch_nsa[l])
                  + g_fox * (o_fox @ w_branch_fox[l])
                  + g_mem_br * (o_mem @ w_branch_mem[l]))
        x = x + merged @ w_out[l]

        x = x + moe_ffn(rms_norm(x, g_ffn[l]), w_router[l], b_router[l], w_gate_up[l],
                        b_gate_up[l], w_down[l], b_down[l])

    return rms_norm(x, g_final)


_drawn_inputs = setup_inputs


def setup_inputs(seed=0):
    import zlib

    import numpy as np

    out = dict(_drawn_inputs(seed))
    spreads = {}
    factors = {'b_merge': 2.997,
     'nsa_pe_k': 200.0,
     'nsa_pe_v': 14.295,
     'g_mem': 4.084,
     'b_gate_up': 5.179,
     'b_down': 5.952,
     'g_final': 22.029,
     'b_router': 2.81}
    for name, (base, spread) in spreads.items():
        noise = np.random.default_rng([zlib.crc32(name.encode()), seed]).standard_normal(out[name].shape)
        drawn = base * np.exp(spread * noise) if base else spread * noise
        out[name] = jnp.asarray(drawn.astype(out[name].dtype))
    for name, factor in factors.items():
        out[name] = (out[name] * factor).astype(out[name].dtype)
    return out
```

```python
from contextlib import ExitStack

import concourse.bass as bass
from concourse import mybir

F32 = mybir.dt.float32
F32R = mybir.dt.float32r
BF16 = mybir.dt.bfloat16
I32 = mybir.dt.int32
U32 = mybir.dt.uint32
ALU = mybir.AluOpType
ACT = mybir.ActivationFunctionType
AX = mybir.AxisListType.X

P = 128
HD = 64
CAP = 64
NEG = -1e30
EPS = 1e-5
LIMIT = 7.0
ALPHA = 1.702


def hybrid_layer(nc, rope, x, mem, g_mix, w_in, b_forget, b_merge, nsa_pe_k, nsa_w1_k, nsa_w2_k, nsa_pe_v,
                 nsa_w1_v, nsa_w2_v, g_mem, w_mem_kv, w_branch_nsa, w_branch_fox, w_branch_mem, w_out,
                 g_ffn, w_router, b_router, w_gate_up, b_gate_up, w_down, b_down, g_final, out):
    _, T, D = x.shape
    KC = D // P
    TB = T // P
    NE = w_gate_up.shape[1]
    F = w_down.shape[2]
    CMP = nsa_pe_k.shape[1]
    STRIDE = CMP // 2
    NCMP = T // STRIDE - 1
    FH = b_forget.shape[1]
    NH = FH
    REP = NH // 2
    MH = w_branch_mem.shape[1] // P
    MT = 3 * D // P
    LEVELS = T // CAP
    SCALE = HD ** -0.5
    MSCALE = P ** -0.5
    assert T == 256 and D == 1024 and NE == 32 and F == D and MH == 4 and NH == 8

    Q_A, K_C, K_W, GL, Q_F, K_F, V_F, F_L, Q_M, MERGE = 0, 512, 1024, 1280, 1304, 1816, 2328, 2840, 2848, 3360

    with ExitStack() as ctx:
        address = {}

        def sb(name, shape, dt=F32):
            address[name] = (nc.sbuf_base + 31) // 32 * 32
            return ctx.enter_context(nc.sbuf_tensor(name, shape, dt))

        def rounded(name, over, first, shape):
            return nc.alloc_sbuf_tensor_at(name, shape, F32R, offset=address[over] + 4 * first)

        def sem(name):
            return ctx.enter_context(nc.semaphore(name))

        ps = ctx.enter_context(nc.psum_tensor("ps", [P, 8, 512], F32))

        ring = sb("ring", [P, 12, 2048])
        NG = 4
        gates = ring[:, 8:11, :].rearrange("p s n -> p (s n)").rearrange("p (m t) -> p m t", t=T)

        def group(i):
            pos = (i + 3) % NG
            return ring[:, 2 * pos:2 * pos + 2, :].rearrange("p s n -> p (s n)")

        ring_high = rounded("ring_high", "ring", 8 * 2048, [P, 4 * 2048])
        ring_low = rounded("ring_low", "ring", 0, [P, 8 * 2048])

        def high_of_stream(i, n):
            return ring_high[:, 4096 * (i % 2):4096 * (i % 2) + KC * n].rearrange("p (c n) -> p c n", c=KC)

        def low_of_stream(i, n=512):
            pos = (i + 3) % NG
            return ring_low[:, 4096 * pos:4096 * pos + KC * n].rearrange("p (c n) -> p c n", c=KC)

        def high_of_tile(m):
            first = 3 * 2048 + 1024 * (m % 2)
            return ring_high[:, first:first + 1024].rearrange("p (c n) -> p c n", c=KC)

        xs = sb("xs", [P, TB, D])
        xn = sb("xn", [P, TB, D])
        hT = sb("hT", [P, KC, T])
        hT_parts = hT_high, _ = rounded("hT_high", "xn", 0, [P, KC, T]), rounded("hT_low", "hT", 0, [P, KC, T])
        mT = sb("mT", [P, KC, T])
        mergedT = mT
        ident = sb("ident", [P, P])
        identb = sb("identb", [P, P], BF16)
        causal = sb("causal", [P, P], BF16)
        cneg = sb("cneg", [P, TB, 1, 16])
        cone = sb("cone", [P, TB, 1, 16])
        triU = sb("triU", [P, T])
        iota_e = sb("iota_e", [P, NE])
        iota_s = sb("iota_s", [P, P])
        rp = sb("rp", [P, TB, 2, HD])
        gains = sb("gains", [P, 3, KC])
        bmrow = sb("bmrow", [MT, P])
        bmerge = sb("bmerge", [P, MT])
        eps = sb("eps", [P, 1])
        flag = sb("flag", [P, 1])
        stats = sb("stats", [P, 3, 8])
        bforget = sb("bforget", [P, 1, FH])
        brouter = sb("brouter", [P, 1, NE])
        wrout = sb("wrout", [P, KC, NE])
        wfl = sb("wfl", [P, KC, FH])
        w2 = sb("w2", [HD, 2, HD])
        pe = sb("pe", [CMP, 2, P])
        peT = sb("peT", [P, 2, CMP])

        early = sb("early", [P, 3072])
        qr = early[:, 0:1024].rearrange("p (b n) -> p b n", b=TB)
        kr = early[:, 1024:2048].rearrange("p (b k n) -> p b k n", b=TB, k=4)
        blk = early[:, 2048:3008].rearrange("p (k l g n) -> p k l g n", k=2, l=STRIDE, g=2)
        oT = early[:, 0:3072].rearrange("p (j t) -> p j t", t=T)
        NX = 4
        extra = sb("extra", [P, NX, 2048])
        space = extra[:, :, :].rearrange("p s n -> p (s n)")
        qfk = space[0:HD + 1, 0:4096].rearrange("p (a h t) -> p a h t", a=2, h=FH)
        qmT = space[:, 4096:5120].rearrange("p (h t) -> p h t", h=MH)
        kmT = space[:, 5120:6144].rearrange("p (h t) -> p h t", h=MH)
        kT = space[:, 6144:7168].rearrange("p (k t) -> p k t", k=4)
        vf = space[:, 7168:8192].rearrange("p (b n) -> p b n", b=TB)
        xrows = space[:, 4096:6144].rearrange("p (b n) -> p b n", b=TB)
        memrows = space[:, 6144:8192].rearrange("p (b n) -> p b n", b=TB)
        mT_parts = mT_high, _ = rounded("mT_high", "extra", 2048, [P, KC, T]), rounded("mT_low", "mT", 0, [P, KC, T])
        attn = sb("attn", [P, 3584])
        vm = attn[:, 0:1024].rearrange("p (b n) -> p b n", b=TB)
        vsw = attn[:, 1024:1536].rearrange("p (b k n) -> p b k n", b=TB, k=2)
        ropet = attn[:, 1536:2560].rearrange("p (a n) -> p a n", a=2)
        glg = sb("glg", [P, TB, 24])
        fz = sb("fz", [P, 4, TB, FH])
        logf = sb("logf", [P, TB, FH])
        cumT = sb("cumT", [FH, T])
        cumtok = sb("cumtok", [P, TB, FH])
        qT = sb("qT", [P, REP, T])
        zt = sb("zt", [HD, 3, 2, 32])
        zs = sb("zs", [HD, 2, 2, 32])
        kcmpT = sb("kcmpT", [P, 16])
        vcmp = sb("vcmp", [P, 2, HD])
        cst = sb("cst", [P, 3, TB, NH, 1])
        pc = sb("pc", [P, TB, NH, 32])
        pcT = sb("pcT", [P, 2, T])
        prob = ropet
        probT = attn[:, 2560:3584].rearrange("p (a n) -> p a n", a=2)
        sc = probT[:, :, 0:TB * NH * 16].rearrange("p k (b h n) -> p k b h n", b=TB, h=NH)
        UN = 28
        st_mx = sb("st_mx", [P, UN, 2])
        st_mf = sb("st_mf", [P, UN, 2])
        st_nb = sb("st_nb", [P, UN, 2])
        st_sum = sb("st_sum", [P, UN, 2])
        st_cl = sb("st_cl", [P, UN, 2])
        st_rc = sb("st_rc", [P, UN, 2])
        st_rg = sb("st_rg", [P, UN, 2])

        late = {"used": 0}
        late_space = qT[:, :, :].rearrange("p r t -> p (r t)")

        def reused(*shape):
            n = 1
            for d in shape:
                n *= d
            flat = late_space[:, late["used"]:late["used"] + n]
            late["used"] += n
            if len(shape) == 1:
                return flat
            return flat.rearrange("p (a b) -> p a b", a=shape[0])

        lg = reused(TB, NE)
        m8 = reused(TB, 8)
        i8 = reused(TB, 8).bitcast(U32)
        idxf = reused(TB, 8)
        nm = reused(TB)
        e4 = reused(TB, 4)
        s4 = reused(TB)
        r4 = reused(TB)
        eq, eqg = (early[:, 1024 + 256 * k:1280 + 256 * k].rearrange("p (b j e) -> p b j e", b=TB, j=4) for k in range(2))
        sel = reused(TB, NE)
        cntf = reused(1)
        posm = sb("posm", [P, TB, NE + 1])
        gtab = sb("gtab", [P, TB, NE + 1])
        cnti = sb("cnti", [P, 1], I32)

        biases = attn[0:NE, 0:3 * F]
        gfin = mT[:, 4:8, :].rearrange("p c t -> p (c t)")
        xT = mT[:, 0:2, :].rearrange("p c t -> p (c t)").rearrange("p (c s) -> p c s", c=KC)
        S = reused(TB, CAP)
        SG = reused(TB, P)
        ST = reused(TB, P)
        oneh = reused(2, CAP)[0:NE]
        gm = early[:, 0:512]
        um = early[:, 512:1024]
        sg = early[:, 1024:1536]
        act = early[:, 1536:2048]
        actT = early[:, 2048:2560]
        oE = early[:, 2560:3072]

        x_in = [sem(f"x_in{b}") for b in range(TB)]
        mem_in, small_in, consts_in, late_in, biases_in = (sem(n) for n in (
            "mem_in", "small_in", "consts_in", "late_in", "biases_in"))
        group_full = [sem(f"group_full{i}") for i in range(NG)]
        group_used = sem("group_used")
        masks_ready, masks_step = sem("masks_ready"), sem("masks_step")
        eps_set, squares, roots, recips, xn_ready = sem("eps_set"), sem("squares"), sem("roots"), sem("recips"), sem("xn_ready")
        xT_done, hT_ready, hT_high_ready, hT_low_ready = (sem(n) for n in (
            "xT_done", "hT_ready", "hT_high_ready", "hT_low_ready"))
        w_high_ready, w_low_ready = sem("w_high_ready"), sem("w_low_ready")
        tile_high_ready, tile_low_ready = sem("tile_high_ready"), sem("tile_low_ready")
        proj_done, rope_done, proj_copied = sem("proj_done"), sem("rope_done"), sem("proj_copied")
        rope_step = sem("rope_step")
        kqT_done, kqT_ready = sem("kqT_done"), sem("kqT_ready")
        wst_done, wst_copied = sem("wst_done"), sem("wst_copied")
        forget_step, forget_act = sem("forget_step"), sem("forget_act")
        cum_done, cum_copied, cum_rows = sem("cum_done"), sem("cum_copied"), sem("cum_rows")
        peT_done, peT_ready, blk_ready = sem("peT_done"), sem("peT_ready"), sem("blk_ready")
        z_done, z_exp, z_step, z_ready = sem("z_done"), sem("z_exp"), sem("z_step"), sem("z_ready")
        cmp_done, cmp_ready = sem("cmp_done"), sem("cmp_ready")
        gl_exp, gl_step = sem("gl_exp"), sem("gl_step")
        sc_done, sc_step, sc_exp, pc_ready, pcT_done, pcT_ready = (sem(n) for n in (
            "sc_done", "sc_step", "sc_exp", "pc_ready", "pcT_done", "pcT_ready"))
        score_done, max_done, bias_step, bias_ready, exp_done = (sem(n) for n in (
            "score_done", "max_done", "bias_step", "bias_ready", "exp_done"))
        norm_step, prob_ready, probT_done, probT_ready = (sem(n) for n in (
            "norm_step", "prob_ready", "probT_done", "probT_ready"))
        heads_done, heads_copied = sem("heads_done"), sem("heads_copied")
        merge_done, merge_exp, gate_step, gate_ready = (sem(n) for n in (
            "merge_done", "merge_exp", "gate_step", "gate_ready"))
        branch_done, branch_read, merged_ready = sem("branch_done"), sem("branch_read"), sem("merged_ready")
        out_done, x2_ready = sem("out_done"), sem("x2_ready")
        router_done, route_step, route_exp, sel_table = (sem(n) for n in (
            "router_done", "route_step", "route_exp", "sel_table"))
        pos_done, tables_ready = sem("pos_done"), sem("tables_ready")
        slot_full = [sem(f"slot_full{i}") for i in range(12)]
        ring_used = sem("ring_used")
        sel_ready, gather_done, xt_ready, sg_ready = (sem(n) for n in (
            "sel_ready", "gather_done", "xt_ready", "sg_ready"))
        ohg_ready, ohd_ready = sem("ohg_ready"), sem("ohd_ready")
        st_done, st_copied, g_clamped, u_clamped, u_times_g = (sem(n) for n in (
            "st_done", "st_copied", "g_clamped", "u_clamped", "u_times_g"))
        sig_ready, act_ready, actT_done, actT_copied = (sem(n) for n in (
            "sig_ready", "act_ready", "actT_done", "actT_copied"))
        out_copied, scatter_done, added = (sem(n) for n in (
            "out_copied", "scatter_done", "added"))
        shifted = sem("shifted")
        final_step, stored = sem("final_step"), sem("stored")

        def w_rows(w, c0, n):
            return w[0].rearrange("(p c) n -> p c n", c=KC)[:, :, c0:c0 + n]

        def w_chunks(w, k0, n0, n):
            return w[0].rearrange("(c p) n -> p c n", p=P)[:, :, n0:n0 + n]

        streams = ([("q_a", w_in, Q_A, 512), ("kvc_kvs", w_in, K_C, 512), ("kvw_gl", w_in, K_W, 280),
                    ("v_f", w_in, V_F, 512), ("m_k", w_mem_kv, 0, 512), ("m_v", w_mem_kv, 512, 512),
                    ("q_f", w_in, Q_F, 512), ("k_f", w_in, K_F, 512), ("q_m", w_in, Q_M, 512),
                    ("w1", None, 0, 0)]
                   + [(f"merge{i}", w_in, MERGE + 512 * i, 512) for i in range(6)]
                   + [("b_nsa", w_branch_nsa, 0, 0), ("b_mem", w_branch_mem, 0, 0), ("b_fox", w_branch_fox, 0, 0),
                      ("out0", w_out, 0, 512), ("out1", w_out, 512, 512)])
        at = {name: i for i, (name, _, _, _) in enumerate(streams)}
        NS = len(streams)

        def wcols(name, n=512):
            return group(at[name])[:, 0:KC * n].rearrange("p (c n) -> p c n", c=KC)

        def arrived(eng, name):
            i = at[name]
            eng.wait_ge(group_full[i % NG], (16 if name != "w1" else 64) + 16 * (i // NG)
                        + (48 if i > at["w1"] and i % NG == at["w1"] % NG else 0))

        def pieces_of(i):
            n = streams[i][3]
            for k in range(KC // 2):
                yield (KC // 2 * i + k, *(w[:, 2 * k:2 * k + 2, :] for w in (
                    wcols(streams[i][0], n), high_of_stream(i, n), low_of_stream(i, n))))

        def merge_cols(m):
            return wcols(f"merge{m // 4}")[:, :, P * (m % 4):P * (m % 4) + P]

        def low_of_tile(m):
            return low_of_stream(at[f"merge{m // 4}"])[:, :, P * (m % 4):P * (m % 4) + P]

        w1 = group(at["w1"])[:, 0:2 * STRIDE * HD].rearrange("p (k l e) -> p k l e", k=2, l=STRIDE)

        z = ps[0:HD, 0, 0:64].rearrange("p (k c) -> p k c", k=2)

        block = ctx.enter_context(nc.Block())

        units = ([("slc" if br == 0 else "win", h) for h in range(NH) for br in range(2)]
                 + [("mem", h) for h in range(MH)] + [("fox", h) for h in range(FH)])
        PRE = 4
        nsa0, mem0, fox0 = MT, MT + KC, MT + 2 * KC
        BRANCH = {nsa0: ("b_nsa", 0, 0), mem0: ("b_mem", 2, 8), fox0: ("b_fox", 1, 4)}

        def tiles_ending(s):
            last = 2 * (MT - PRE) // 2
            return [PRE + s] if s < last else [nsa0 + 2 * (s - last) + k for k in range(2)] if s < len(units) else []

        def nsa_gate(kind, h):
            return glg[:, :, 3 * h + {"cmp": 0, "slc": 1, "win": 2}[kind]]

        closing = {u: (u // 4 if k in ("slc", "win") else 4 + h // 2 if k == "fox" else 8 + h)
                   for u, (k, h) in enumerate(units)
                   if (k == "win" and h % 2) or (k == "fox" and h % 2) or k == "mem"}
        closed = {}
        for u in sorted(closing):
            closed[u] = len(closed)

        @block.sync
        def _(sp):
            for b in range(TB):
                sp.dma_start(xs[:, b, :], x[0, P * b:P * b + P, :]).then_inc(x_in[b], 16)
            for i, (name, w, c0, n) in enumerate(streams):
                if i == 1:
                    sp.dma_start(memrows, mem[0].rearrange("(b p) n -> p b n", p=P)).then_inc(mem_in, 16)
                if i >= NG:
                    sp.wait_ge(group_used, i - NG + 1)
                full = group_full[i % NG]
                if name == "w1":
                    for half in range(2):
                        for kv, wk in enumerate((nsa_w1_k, nsa_w1_v)):
                            sp.dma_start(w1[HD * half:HD * half + HD, kv],
                                         wk[0, STRIDE * half:STRIDE * half + STRIDE].rearrange("l d e -> d l e")
                                         ).then_inc(full, 16)
                elif name[0:2] == "b_":
                    sp.dma_start(group(i).rearrange("p (c n) -> p c n", c=4),
                                 w[0].rearrange("(c p) n -> p c n", p=P)).then_inc(full, 16)
                elif name[0:3] == "out":
                    sp.dma_start(wcols(name), w[0].rearrange("(c p) n -> p c n", p=P)[:, :, c0:c0 + n]
                                 ).then_inc(full, 16)
                else:
                    sp.dma_start(wcols(name, n), w_rows(w, c0, n)).then_inc(full, 16)

            def slot_load(s, e, dst=None):
                if s < KC:
                    src = w_gate_up[0, bass.ds(e, 1)].rearrange("a (p c) n -> (a p) c n", c=KC)[:, s, :]
                else:
                    h, q = (s - KC) // 2, (s - KC) % 2
                    src = w_down[0, bass.ds(e, 1)].rearrange("a (h m r) n -> (a m) h (r n)", h=2, r=4
                                                              )[:, h, 2048 * q:2048 * q + 2048]
                sp.dma_start(ring[:, s, :] if dst is None else dst, src).then_inc(slot_full[s], 16)

            sp.wait_ge(heads_done, len(closed))
            for s in range(NX):
                slot_load(s, 0, extra[:, s, :])
            sp.wait_ge(merged_ready, 2 * KC)
            for s in range(KC, 12):
                slot_load(s, 0)
            for s in range(NX, KC):
                sp.wait_ge(group_used, NS - NG + s // 2 + 1)
                slot_load(s, 0)
            for s in range(NX):
                sp.wait_ge(slot_full[s], 16)
                slot_load(s, 1)

            def item(level, e, start=0):
                for s in range(start, 12):
                    sp.wait_ge(ring_used, 12 * (NE * level + e - 1) + s + 1)
                    slot_load(s, e)

            item(0, 1, NX)
            with sp.Fori(2, NE) as e:
                item(0, e)
            sp.wait_ge(tables_ready, 1)
            most = sp.value_load(cnti[0:1, 0:1], min_val=0, max_val=T)
            with sp.If(most > CAP):
                with sp.Fori(1, LEVELS) as level:
                    with sp.Fori(0, NE) as e:
                        item(level, e)
            for b in range(TB):
                sp.wait_ge(final_step, 2 * b + 3)
                sp.dma_start(out[0, P * b:P * b + P, :], xs[:, b, :]).then_inc(stored, 16)
            sp.wait_ge(stored, 16 * TB)

        @block.gpsimd
        def _(pool):
            pool.memset(ident[:], 0.0).then_inc(masks_step, 1)
            pool.memset(identb[:], 0.0).then_inc(masks_step, 1)
            pool.memset(causal[:], 0.0).then_inc(masks_step, 1)
            pool.memset(cneg[:], 0.0).then_inc(masks_step, 1)
            pool.memset(cone[:], 1.0).then_inc(masks_step, 1)
            pool.memset(triU[:], 1.0).then_inc(masks_step, 1)
            pool.wait_ge(masks_step, 6)
            for m in (ident, identb):
                pool.affine_select(out=m[:], in_=m[:], compare_op=ALU.not_equal, fill=1.0, base=0,
                                   pattern=[[-1, P]], channel_multiplier=1).then_inc(masks_ready, 1)
            pool.memset(zs[:], 0.0).then_inc(masks_ready, 1)
            pool.memset(pc[:], 0.0).then_inc(masks_ready, 1)
            pool.wait_ge(masks_ready, 4)
            pool.memset(qfk[HD:HD + 1, 0], 1.0).then_inc(masks_ready, 1)
            pool.wait_ge(masks_ready, 5)
            pool.affine_select(out=causal[:], in_=causal[:], compare_op=ALU.is_ge, fill=NEG, base=0,
                               pattern=[[-1, P]], channel_multiplier=1).then_inc(masks_ready, 1)
            for b in range(TB):
                for m, fill in ((cneg, NEG), (cone, 0.0)):
                    pool.affine_select(out=m[:, b, 0, :], in_=m[:, b, 0, :], compare_op=ALU.is_ge, fill=fill,
                                       base=P * b - (CMP - 1), pattern=[[-STRIDE, 16]], channel_multiplier=1
                                       ).then_inc(masks_ready, 1)
            pool.affine_select(out=triU[:, 0:P], in_=triU[:, 0:P], compare_op=ALU.is_ge, fill=0.0, base=0,
                               pattern=[[1, P]], channel_multiplier=-1).then_inc(masks_ready, 1)
            pool.iota(iota_e[:], pattern=[[1, NE]], base=0, channel_multiplier=0,
                      allow_small_or_imprecise_dtypes=True).then_inc(masks_ready, 1)
            pool.iota(iota_s[:], pattern=[[0, 2], [1, CAP]], base=0, channel_multiplier=0,
                      allow_small_or_imprecise_dtypes=True).then_inc(masks_ready, 1)
            pool.memset(posm[:], -1.0).then_inc(masks_ready, 1)
            pool.memset(gtab[:], 0.0).then_inc(masks_ready, 1)

        @block.scalar
        def _(a):
            for g, w in enumerate((g_mix, g_mem, g_ffn)):
                a.dma_start(gains[:, g, :], w[0].rearrange("(p c) -> p c", c=KC)).then_inc(small_in, 16)
            a.dma_start(rp[:], rope.rearrange("(b p) (k n) -> p b k n", p=P, k=2)).then_inc(small_in, 16)
            a.dma_start(wfl[:], w_rows(w_in, F_L, FH)).then_inc(consts_in, 16)
            a.dma_start(bforget[:, 0, :], b_forget[0].partition_broadcast(P)).then_inc(consts_in, 16)
            a.dma_start(bmrow[:], b_merge[0].rearrange("(m p) -> m p", p=P)).then_inc(consts_in, 16)
            for kv, (wk, pk) in enumerate(((nsa_w2_k, nsa_pe_k), (nsa_w2_v, nsa_pe_v))):
                a.dma_start(w2[:, kv, :], wk[0]).then_inc(consts_in, 16)
                for half in range(2):
                    a.dma_start(pe[:, kv, HD * half:HD * half + HD], pk[0]).then_inc(consts_in, 16)
            a.dma_start(wrout[:], w_rows(w_router, 0, NE)).then_inc(late_in, 16)
            a.dma_start(brouter[:, 0, :], b_router[0].partition_broadcast(P)).then_inc(late_in, 16)

            scr = early[:, 0:D]

            def square_root_of(src, b, k):
                a.activation(scr, src[:, b, :], ACT.Square, accum_out=stats[:, 0, k:k + 1]).then_inc(squares, 1)
                a.wait_ge(squares, k + 1)
                a.activation(stats[:, 1, k:k + 1], stats[:, 0, k:k + 1], ACT.Sqrt, scale=1.0 / D, bias=eps[:, 0:1]
                             ).then_inc(roots, 1)

            def high_of(i):
                arrived(a, streams[i][0])
                if i >= 2:
                    a.wait_ge(group_used, i - 1)
                for _, raw, high, _ in pieces_of(i):
                    a.activation(high, raw, ACT.Copy).then_inc(w_high_ready, 1)

            def high_of_hT(src, dst, task):
                b, half = task // 2 % 2, task % 2
                part = (slice(None), slice(4 * half, 4 * half + 4), slice(P * b, P * b + P))
                a.wait_ge(hT_ready, task + 1)
                a.activation(dst[part], src[part], ACT.Copy).then_inc(hT_high_ready, 1)

            a.wait_ge(eps_set, 1)
            for b in range(TB):
                a.wait_ge(x_in[b], 16)
                square_root_of(xs, b, b)
            high_of(0)
            for t in range(4):
                high_of_hT(hT, hT_high, t)
            a.wait_ge(mem_in, 16)
            for b in range(TB):
                square_root_of(memrows, b, 2 + b)
            high_of(1)
            high_of(2)
            for t in range(4, 8):
                high_of_hT(mT, mT_high, t)

            for b in range(TB):
                a.wait_ge(proj_done, 3 + b)
                a.activation(kr[:, b, 3, :], ps[:, 2 + b, 128:256], ACT.Copy).then_inc(proj_copied, 1)
                a.activation(vsw[:, b, 0, :], ps[:, 2 + b, 384:512], ACT.Copy).then_inc(proj_copied, 1)
            high_of(3)
            for b in range(TB):
                a.wait_ge(proj_done, 5 + b)
                a.activation(vsw[:, b, 1, :], ps[:, b, 128:256], ACT.Copy).then_inc(proj_copied, 1)
                a.activation(glg[:, b, :], ps[:, b, 256:280], ACT.Exp, scale=-1.0).then_inc(gl_exp, 1)
            high_of(4)
            for b in range(TB):
                a.wait_ge(proj_done, 7 + b)
                a.activation(vf[:, b, :], ps[:, 2 + b, :], ACT.Copy).then_inc(proj_copied, 1)
            high_of(5)
            for b in range(TB):
                a.wait_ge(kqT_done, 1 + b)
                a.activation(qT[:, :, P * b:P * b + P], ps[:, b, :].rearrange("p (r t) -> p r t", r=REP), ACT.Copy
                             ).then_inc(kqT_ready, 1)
            for b in range(TB):
                a.wait_ge(kqT_done, 3 + b)
                a.activation(kT[:, :, P * b:P * b + P], ps[:, 2 + b, :].rearrange("p (k t) -> p k t", k=4), ACT.Copy
                             ).then_inc(kqT_ready, 1)
            a.wait_ge(forget_step, 3)
            a.activation(fz[:, 2], fz[:, 1], ACT.Exp, scale=-1.0).then_inc(forget_act, 1)
            a.wait_ge(forget_act, 1)
            a.activation(fz[:, 3], fz[:, 2], ACT.Ln, bias=1.0).then_inc(forget_act, 1)

            for t in range(10):
                a.wait_ge(wst_done, t + 1)
                bank = ps[:, 4 + t % 4, :]
                pair = bank.rearrange("p (j t) -> p j t", j=2)
                kind, half = t // 2, t % 2
                if kind == 0:
                    a.activation(kmT[:, 2 * half:2 * half + 2, :], pair, ACT.Copy).then_inc(wst_copied, 1)
                elif kind == 1:
                    a.activation(vm[:, half, :], bank, ACT.Copy).then_inc(wst_copied, 1)
                elif kind == 4:
                    a.activation(qmT[:, 2 * half:2 * half + 2, :], pair, ACT.Copy).then_inc(wst_copied, 1)
                else:
                    for odd in range(2):
                        heads = qfk[0:HD, kind - 2, 4 * half + odd:4 * half + odd + 3:2, :]
                        i = a.activation(heads, pair[HD * odd:HD * odd + HD], ACT.Copy)
                    i.then_inc(wst_copied, 1)
                if t == 3:
                    a.wait_ge(cum_done, 1)
                    a.activation(cumT[:], ps[0:FH, 0, 0:T], ACT.Copy, scale=-1.0 / SCALE).then_inc(cum_copied, 1)
                    a.activation(cumtok[:], ps[:, 1, 0:TB * FH].rearrange("p (b h) -> p b h", b=TB), ACT.Copy
                                 ).then_inc(cum_copied, 1)
                    a.wait_ge(cum_copied, 1)
                    for h in range(FH):
                        a.dma_start(qfk[HD:HD + 1, 1, h, :], cumT[h:h + 1, :]).then_inc(cum_rows, 16)
                    a.wait_ge(peT_done, 1)
                    a.activation(peT[:], ps[:, 2, 0:2 * CMP].rearrange("p (k l) -> p k l", k=2), ACT.Copy
                                 ).then_inc(peT_ready, 1)
                    a.activation(bmerge[:], ps[:, 2, 2 * CMP:2 * CMP + MT], ACT.Copy, scale=-1.0
                                 ).then_inc(peT_ready, 1)
                if t in (1, 3, 5):
                    high_of(6 + t // 2)

            def high_of_merge(m):
                if m % 4 == 0:
                    arrived(a, f"merge{m // 4}")
                if m >= 2:
                    a.wait_ge(merge_done, m - 1)
                a.activation(high_of_tile(m), merge_cols(m), ACT.Copy).then_inc(tile_high_ready, 1)

            def gate_exp(m):
                a.wait_ge(merge_done, m + 1)
                a.activation(gates[:, m, :], ps[:, 6 + m % 2, 0:T], ACT.Exp, scale=-1.0, bias=bmerge[:, m:m + 1]
                             ).then_inc(merge_exp, 1)
                if m + 2 < MT:
                    high_of_merge(m + 2)

            a.wait_ge(group_used, at["k_f"] + 1)
            high_of_merge(0)
            high_of_merge(1)
            a.wait_ge(peT_ready, 2)
            a.wait_ge(z_done, 1)
            a.activation(zt[:, 0, :, 0:2 * NCMP], z[:, :, 0:2 * NCMP], ACT.Exp, scale=-1.0).then_inc(z_exp, 1)
            gate_exp(0)
            a.wait_ge(cmp_done, 1)
            a.activation(kcmpT[:, 0:NCMP], ps[:, 2, 0:NCMP], ACT.Copy).then_inc(cmp_ready, 1)
            a.activation(vcmp[:], ps[:, 3, 0:2 * HD].rearrange("p (g d) -> p g d", g=2), ACT.Copy
                         ).then_inc(cmp_ready, 1)
            gate_exp(1)
            a.wait_ge(sc_step, 3)
            a.activation(sc[:, 1, :, :, 0:NCMP], sc[:, 0, :, :, 0:NCMP], ACT.Exp, scale=SCALE).then_inc(sc_exp, 1)
            gate_exp(2)
            gate_exp(3)
            a.wait_ge(pcT_done, 1)
            a.activation(pcT[:], ps[:, 2, :].rearrange("p (q t) -> p q t", q=2), ACT.Copy).then_inc(pcT_ready, 1)

            for s in range(len(units) + 1):
                if s < len(units):
                    kind, h = units[s]
                    a.wait_ge(bias_ready, s + 1)
                    if s >= 2:
                        a.wait_ge(probT_done, s - 1)
                    bank = ps[:, s % 2, :]
                    scale = MSCALE if kind == "mem" else SCALE
                    cols = ((0, 256), (256, 512)) if kind == "mem" else ((0, 128), (128, 384))
                    for q, (c0, c1) in enumerate(cols):
                        i = a.activation(prob[:, s % 2, c0:c1], bank[:, c0:c1], ACT.Exp, scale=scale,
                                         bias=st_nb[:, s, q:q + 1], accum_out=st_sum[:, s, q:q + 1])
                    i.then_inc(exp_done, 1)
                if s >= 1:
                    a.wait_ge(probT_done, s)
                    n = 512 if units[s - 1][0] == "mem" else 384
                    a.activation(probT[:, (s - 1) % 2, 0:n], ps[:, 2 + (s - 1) % 2, 0:n], ACT.Copy
                                 ).then_inc(probT_ready, 1)
                for m in tiles_ending(s):
                    if m < MT:
                        gate_exp(m)
                for u in ([s - 2] if s < len(units) else [s - 2, s - 1]):
                    if u in closing:
                        a.wait_ge(heads_done, closed[u] + 1)
                        a.activation(oT[:, closing[u], :], ps[:, 4 + closed[u] % 2, 0:T], ACT.Copy
                                     ).then_inc(heads_copied, 1)
            a.wait_ge(heads_done, len(closed))
            a.dma_start(biases[:, 0:2 * F], b_gate_up[0]).then_inc(biases_in, 16)
            a.dma_start(biases[:, 2 * F:3 * F], b_down[0]).then_inc(biases_in, 16)

            for b in range(TB):
                a.wait_ge(x2_ready, 2 * b + 2)
                square_root_of(xs, b, 4 + b)
            a.wait_ge(out_done, 2 * TB)
            a.dma_start(gfin, g_final.partition_broadcast(P)).then_inc(biases_in, 16)
            a.wait_ge(route_step, 5)
            for b in range(TB):
                a.activation(e4[:, b, :], m8[:, b, 0:4], ACT.Exp, bias=nm[:, b:b + 1], accum_out=s4[:, b:b + 1]
                             ).then_inc(route_exp, 1)

            def item(level, e):
                n = NE * level + e
                a.wait_ge(g_clamped, n + 1)
                a.activation(sg, gm, ACT.Sigmoid, scale=ALPHA).then_inc(sig_ready, 1)
                a.wait_ge(st_done, n + 1)
                a.activation(ST, ps[:, 4, 0:TB * P].rearrange("p (b t) -> p b t", b=TB), ACT.Copy
                             ).then_inc(st_copied, 1)
                a.wait_ge(actT_done, n + 1)
                a.activation(actT, ps[:, 3, :], ACT.Copy).then_inc(actT_copied, 1)
                a.wait_ge(ring_used, 12 * n + 12)
                a.activation(oE, ps[:, 5, :], ACT.Copy).then_inc(out_copied, 1)

            a.wait_ge(tables_ready, 1)
            most = a.value_load(cnti[0:1, 0:1], min_val=0, max_val=T)
            with a.Fori(0, NE) as e:
                item(0, e)
            with a.If(most > CAP):
                with a.Fori(1, LEVELS) as level:
                    with a.Fori(0, NE) as e:
                        item(level, e)
            for b in range(TB):
                a.wait_ge(final_step, 1)
                square_root_of(xs, b, 6 + b)

        @block.vector
        def _(v):
            v.memset(eps[:], EPS).then_inc(eps_set, 1)

            def normalise(src, b, k, dst):
                v.wait_ge(roots, k + 1)
                v.reciprocal(stats[:, 2, k:k + 1], stats[:, 1, k:k + 1]).then_inc(recips, 1)
                v.wait_ge(recips, k + 1)
                return v.tensor_scalar(dst[:, b, :], src[:, b, :], stats[:, 2, k:k + 1], None, ALU.mult)

            for b in range(TB):
                normalise(xs, b, b, xrows).then_inc(xn_ready, 1)
            v.wait_ge(masks_ready, 15)

            def to_hT(dst, g, task, bank):
                b, half = task // 2 % 2, task % 2
                v.wait_ge(xT_done, task + 1)
                v.tensor_tensor(dst[:, 4 * half:4 * half + 4, P * b:P * b + P],
                                ps[:, bank, :].rearrange("p (c t) -> p c t", c=4),
                                gains[:, g, 4 * half:4 * half + 4].unsqueeze(2).to_broadcast([P, 4, P]), ALU.mult
                                ).then_inc(hT_ready, 1)

            def low_of_hT(parts, raw, task):
                b, half = task // 2 % 2, task % 2
                high, low, raw = (m[:, 4 * half:4 * half + 4, P * b:P * b + P] for m in (*parts, raw))
                v.wait_ge(hT_high_ready, task + 1)
                v.tensor_tensor(low, raw, high.bitcast(F32), ALU.subtract).then_inc(hT_low_ready, 1)

            def low_of(i):
                for n, raw, high, low in pieces_of(i):
                    v.wait_ge(w_high_ready, n + 1)
                    v.tensor_tensor(low, raw, high.bitcast(F32), ALU.subtract).then_inc(w_low_ready, 1)

            def low_of_merge(m):
                v.wait_ge(tile_high_ready, m + 1)
                v.tensor_tensor(low_of_tile(m), merge_cols(m), high_of_tile(m).bitcast(F32), ALU.subtract
                                ).then_inc(tile_low_ready, 1)

            v.wait_ge(small_in, 64)
            for t in range(4):
                to_hT(hT, 0, t, t)
            for t in range(4):
                low_of_hT(hT_parts, hT, t)
            low_of(0)
            for b in range(TB):
                normalise(memrows, b, 2 + b, memrows).then_inc(xn_ready, 1)
            low_of(1)

            nrope = [0]

            def roped(src, dst, b, n):
                t0 = ropet[:, 0, 0:n * HD].rearrange("p (h d) -> p h d", h=n)
                t1 = ropet[:, 1, 0:n * HD].rearrange("p (h d) -> p h d", h=n)
                hf = HD // 2
                cos = rp[:, b, 0:1, :].to_broadcast([P, n, HD])
                if nrope[0]:
                    v.wait_ge(rope_step, 4 * nrope[0])
                v.tensor_tensor(t0, src, cos, ALU.mult).then_inc(rope_step, 1)
                v.tensor_tensor(t1[:, :, 0:hf], src[:, :, hf:HD],
                                rp[:, b, 1:2, 0:hf].to_broadcast([P, n, hf]), ALU.mult).then_inc(rope_step, 1)
                v.tensor_tensor(t1[:, :, hf:HD], src[:, :, 0:hf],
                                rp[:, b, 1:2, hf:HD].to_broadcast([P, n, hf]), ALU.mult).then_inc(rope_step, 1)
                v.wait_ge(rope_step, 4 * nrope[0] + 3)
                if n == NH:
                    t0, t1 = (m.rearrange("p (g r) d -> p g r d", g=2) for m in (t0, t1))
                v.tensor_tensor(dst, t0, t1, ALU.add).then_inc(rope_step, 1)
                nrope[0] += 1

            def heads_of(ap, n):
                return ap.rearrange("p (h d) -> p h d", h=n)

            v.wait_ge(squares, 4)
            for b in range(TB):
                v.wait_ge(proj_done, 1 + b)
                roped(heads_of(ps[:, b, :], NH), qr[:, b, :].rearrange("p (r g d) -> p g r d", r=REP, g=2), b, NH)
            for t in range(4, 8):
                to_hT(mT, 1, t, t)
            low_of(2)
            for t in range(4, 8):
                low_of_hT(mT_parts, mT, t)
            for b in range(TB):
                v.wait_ge(proj_copied, 2 * (b + 1))
                roped(heads_of(ps[:, 2 + b, 0:128], 2), heads_of(kr[:, b, 2, :], 2), b, 2)
                roped(heads_of(ps[:, 2 + b, 256:384], 2), heads_of(kr[:, b, 0, :], 2), b, 2)
            low_of(3)
            for b in range(TB):
                v.wait_ge(gl_exp, 1 + b)
                roped(heads_of(ps[:, b, 0:128], 2), heads_of(kr[:, b, 1, :], 2), b, 2)
            low_of(4)
            v.wait_ge(consts_in, 16 * 9)
            v.wait_ge(proj_done, 9)
            v.tensor_tensor(fz[:, 0], ps[:, 4, 0:TB * FH].rearrange("p (b h) -> p b h", b=TB),
                            bforget[:].to_broadcast([P, TB, FH]), ALU.add).then_inc(forget_step, 1)
            v.wait_ge(forget_step, 1)
            v.tensor_scalar(fz[:, 2], fz[:, 0], -1.0, None, ALU.mult).then_inc(forget_step, 1)
            v.wait_ge(forget_step, 2)
            v.tensor_tensor(fz[:, 1], fz[:, 0], fz[:, 2], ALU.max).then_inc(forget_step, 1)
            low_of(5)
            v.wait_ge(gl_exp, 2)
            v.tensor_scalar(glg[:], glg[:], 1.0, None, ALU.add).then_inc(gl_step, 1)
            v.wait_ge(gl_step, 1)
            v.reciprocal(glg[:], glg[:]).then_inc(gl_step, 1)
            v.wait_ge(forget_act, 2)
            v.scalar_tensor_tensor(logf[:], fz[:, 0], 0.0, fz[:, 3], ALU.min, ALU.subtract).then_inc(forget_step, 1)
            def gate_of_tile(m):
                v.wait_ge(merge_exp, m + 1)
                v.tensor_scalar(gates[:, m, :], gates[:, m, :], 1.0, None, ALU.add).then_inc(gate_step, 1)
                v.wait_ge(gate_step, m + 1)
                v.reciprocal(gates[:, m, :], gates[:, m, :]).then_inc(gate_ready, 1)

            def branch_of_tile(m):
                k, j = (m - MT) // KC, (m - MT) % KC
                gate = gates[:, KC * (0, 2, 1)[k] + j, :]
                v.wait_ge(branch_done, m - MT + 1)
                if k == 0:
                    v.wait_ge(gate_ready, MT)
                    v.tensor_tensor(mergedT[:, j, :], ps[:, 6 + m % 2, 0:T], gate, ALU.mult).then_inc(branch_read, 1)
                    return
                v.tensor_tensor(gate, ps[:, 6 + m % 2, 0:T], gate, ALU.mult).then_inc(branch_read, 1)
                v.wait_ge(branch_read, m - MT + 1)
                v.tensor_tensor(mergedT[:, j, :], mergedT[:, j, :], gate, ALU.add).then_inc(merged_ready, 1)
                v.wait_ge(merged_ready, m - MT - KC + 1)

            low_of(6)
            v.wait_ge(peT_ready, 1)
            v.wait_ge(kqT_ready, 4)
            for kv in range(2):
                for half in range(2):
                    for g in range(2):
                        rows = slice(HD * g, HD * g + HD)
                        places = slice(STRIDE * half, STRIDE * half + STRIDE)
                        src = kT[rows, 2 + kv, STRIDE * half:STRIDE * half + STRIDE * NCMP]
                        v.tensor_tensor(blk[HD * half:HD * half + HD, kv, :, g, :],
                                        src.rearrange("p (n l) -> p l n", l=STRIDE),
                                        peT[rows, kv, places].unsqueeze(2).to_broadcast([HD, STRIDE, NCMP]), ALU.add
                                        ).then_inc(blk_ready, 1)
            low_of(7)
            low_of(8)
            low_of_merge(0)
            low_of_merge(1)
            v.wait_ge(z_exp, 1)
            v.tensor_scalar(zt[:, 1, :, 0:2 * NCMP], zt[:, 0, :, 0:2 * NCMP], 1.0, None, ALU.add).then_inc(z_step, 1)
            v.wait_ge(z_step, 1)
            v.reciprocal(zt[:, 2, :, 0:2 * NCMP], zt[:, 1, :, 0:2 * NCMP]).then_inc(z_step, 1)
            v.wait_ge(z_step, 2)
            for kv in range(2):
                i = v.tensor_tensor(zs[:, kv, :, 0:NCMP], z[:, kv, 0:2 * NCMP].rearrange("p (g n) -> p g n", g=2),
                                    zt[:, 2, kv, 0:2 * NCMP].rearrange("p (g n) -> p g n", g=2), ALU.mult)
            i.then_inc(z_ready, 1)
            gate_of_tile(0)
            low_of_merge(2)
            gate_of_tile(1)
            low_of_merge(3)
            v.wait_ge(sc_done, 1)
            scm, sce = sc[:, 0, :, :, 0:NCMP], sc[:, 1, :, :, 0:NCMP]
            wide = [P, TB, NH, NCMP]
            for g in range(2):
                raw = ps[:, g, 0:TB * REP * 16].rearrange("p (b r n) -> p b r n", b=TB, r=REP)[:, :, :, 0:NCMP]
                i = v.tensor_tensor(scm[:, :, REP * g:REP * g + REP, :], raw,
                                    cneg[:, :, :, 0:NCMP].to_broadcast([P, TB, REP, NCMP]), ALU.add)
            i.then_inc(sc_step, 1)
            v.wait_ge(sc_step, 1)
            v.tensor_reduce(cst[:, 0], scm, AX, ALU.max).then_inc(sc_step, 1)
            v.wait_ge(sc_step, 2)
            v.tensor_tensor(scm, scm, cst[:, 0].to_broadcast(wide), ALU.subtract).then_inc(sc_step, 1)
            v.wait_ge(sc_exp, 1)
            v.tensor_tensor(sce, sce, cone[:, :, :, 0:NCMP].to_broadcast(wide), ALU.mult).then_inc(sc_step, 1)
            v.wait_ge(sc_step, 4)
            v.tensor_reduce(cst[:, 1], sce, AX, ALU.add).then_inc(sc_step, 1)
            v.wait_ge(sc_step, 5)
            v.tensor_scalar(cst[:, 1], cst[:, 1], 1e-30, None, ALU.max).then_inc(sc_step, 1)
            v.wait_ge(sc_step, 6)
            v.reciprocal(cst[:, 2], cst[:, 1]).then_inc(sc_step, 1)
            v.wait_ge(sc_step, 7)
            v.tensor_tensor(cst[:, 1, :, :, 0], cst[:, 2, :, :, 0],
                            glg[:].rearrange("p b (h k) -> p b h k", k=3)[:, :, :, 0], ALU.mult).then_inc(sc_step, 1)
            v.wait_ge(sc_step, 8)
            v.tensor_tensor(pc[:, :, :, 0:NCMP], sce, cst[:, 1].to_broadcast(wide), ALU.mult).then_inc(pc_ready, 1)
            gate_of_tile(2)
            low_of_merge(4)

            nstep = [0, 0]
            nmax = 0
            v.wait_ge(cum_copied, 2)
            for s in range(len(units) + 1):
                if s < len(units):
                    kind, h = units[s]
                    v.wait_ge(score_done, s + 1)
                    bank = ps[:, s % 2, :]
                    if kind == "mem":
                        v.tensor_reduce(st_mx[:, s, :], bank.rearrange("p (q k) -> p q k", q=2), AX, ALU.max
                                        ).then_inc(max_done, 1)
                        nmax += 1
                    else:
                        v.reduce_max(st_mx[:, s, 0:1], bank[:, 0:128], AX).then_inc(max_done, 1)
                        v.reduce_max(st_mx[:, s, 1:2], bank[:, 128:384], AX).then_inc(max_done, 1)
                        nmax += 2
                    v.wait_ge(max_done, nmax)
                    if kind == "fox":
                        v.scalar_tensor_tensor(st_mf[:, s, :], st_mx[:, s, :], SCALE, cumtok[:, :, h],
                                               ALU.mult, ALU.add).then_inc(bias_step, 1)
                        nstep[0] += 1
                        v.wait_ge(bias_step, nstep[0])
                        v.tensor_tensor(st_nb[:, s, :], cumtok[:, :, h], st_mf[:, s, :], ALU.subtract
                                        ).then_inc(bias_ready, 1)
                    else:
                        v.tensor_scalar(st_nb[:, s, :], st_mx[:, s, :], -(MSCALE if kind == "mem" else SCALE), None,
                                        ALU.mult).then_inc(bias_ready, 1)
                tile = tiles_ending(s - 1)[-1] if s else PRE - 1
                gate_of_tile(tile) if tile < MT else branch_of_tile(tile)
                if s < len(units):
                    u = s
                    kind, h = units[u]
                    v.wait_ge(exp_done, u + 1)
                    total = st_sum[:, u, :]
                    if kind != "mem":
                        v.tensor_scalar(st_cl[:, u, :], total, 1e-30, None, ALU.max).then_inc(norm_step, 1)
                        nstep[1] += 1
                        v.wait_ge(norm_step, nstep[1])
                        total = st_cl[:, u, :]
                    v.reciprocal(st_rc[:, u, :], total).then_inc(norm_step, 1)
                    nstep[1] += 1
                    v.wait_ge(norm_step, nstep[1])
                    factor = st_rc
                    if kind in ("slc", "win"):
                        v.tensor_tensor(st_rg[:, u, :], st_rc[:, u, :], nsa_gate(kind, h), ALU.mult
                                        ).then_inc(norm_step, 1)
                        nstep[1] += 1
                        v.wait_ge(norm_step, nstep[1])
                        factor = st_rg
                    cols = ((0, 256), (256, 512)) if kind == "mem" else ((0, 128), (128, 384))
                    for q, (c0, c1) in enumerate(cols):
                        i = v.tensor_scalar(prob[:, u % 2, c0:c1], prob[:, u % 2, c0:c1], factor[:, u, q:q + 1], None,
                                            ALU.mult)
                    i.then_inc(prob_ready, 1)
                    if PRE + s + 1 < MT:
                        low_of_merge(PRE + s + 1)
                    if len(tiles_ending(s)) == 2:
                        branch_of_tile(tiles_ending(s)[0])

            for m in range(fox0, fox0 + KC):
                branch_of_tile(m)
            for b in range(TB):
                for half in range(b, 2):
                    v.wait_ge(out_done, 2 * b + half + 1)
                    cols = slice(512 * half, 512 * half + 512)
                    v.tensor_tensor(xs[:, b, cols], ps[:, 2 * b + half, :], xs[:, b, cols], ALU.add
                                    ).then_inc(x2_ready, 1)
                normalise(xs, b, 4 + b, xn).then_inc(xn_ready, 1)
                if b == 0:
                    v.wait_ge(out_done, 3)
                    v.tensor_tensor(xs[:, 1, 0:512], ps[:, 2, :], xs[:, 1, 0:512], ALU.add).then_inc(x2_ready, 1)
                for t in range(8 + 2 * b, 10 + 2 * b):
                    to_hT(hT, 2, t, t - 4)

            v.wait_ge(late_in, 32)
            v.wait_ge(router_done, 1)
            v.tensor_tensor(lg, ps[:, 0, 0:TB * NE].rearrange("p (b e) -> p b e", b=TB),
                            brouter[:].to_broadcast([P, TB, NE]), ALU.add).then_inc(route_step, 1)
            v.wait_ge(route_step, 1)
            for b in range(TB):
                v.max(m8[:, b, :], lg[:, b, :]).then_inc(route_step, 1)
            v.wait_ge(route_step, 3)
            v.tensor_scalar(nm, m8[:, :, 0], -1.0, None, ALU.mult).then_inc(route_step, 1)
            for b in range(TB):
                i = v.max_index(i8[:, b, :], m8[:, b, :], lg[:, b, :])
            i.then_inc(route_step, 1)
            v.wait_ge(route_step, 5)
            v.tensor_copy(idxf, i8).then_inc(route_step, 1)
            v.wait_ge(route_step, 6)
            four = [P, TB, 4, NE]
            for b in range(TB):
                i = v.tensor_tensor(eq[:, b], iota_e[:].unsqueeze(1).to_broadcast([P, 4, NE]),
                                    idxf[:, b, 0:4].unsqueeze(2).to_broadcast([P, 4, NE]), ALU.is_equal)
            i.then_inc(route_step, 1)
            v.wait_ge(route_step, 7)
            v.tensor_reduce(sel, eq.rearrange("p b j e -> p b e j"), AX, ALU.add).then_inc(sel_table, 1)
            v.wait_ge(route_exp, 2)
            v.reciprocal(r4, s4).then_inc(route_step, 1)
            v.wait_ge(route_step, 8)
            v.tensor_tensor(e4, e4, r4.unsqueeze(2).to_broadcast([P, TB, 4]), ALU.mult
                            ).then_inc(route_step, 1)
            v.wait_ge(route_step, 9)
            for b in range(TB):
                i = v.tensor_tensor(eqg[:, b], eq[:, b], e4[:, b, :].unsqueeze(2).to_broadcast([P, 4, NE]), ALU.mult)
            i.then_inc(route_step, 1)
            v.wait_ge(route_step, 10)
            v.wait_ge(masks_ready, 15)
            v.tensor_reduce(gtab[:, :, 0:NE], eqg.rearrange("p b j e -> p b e j"), AX, ALU.add
                            ).then_inc(route_step, 1)
            v.wait_ge(pos_done, 1)
            v.tensor_tensor(posm[:, :, 0:NE], ps[:, 1, 0:TB * NE].rearrange("p (b e) -> p b e", b=TB), sel, ALU.mult
                            ).then_inc(route_step, 1)
            v.reduce_max(cntf, ps[:, 1, TB * NE:(TB + 1) * NE], AX).then_inc(route_step, 1)
            v.wait_ge(route_step, 13)
            v.tensor_scalar(posm[:, :, 0:NE], posm[:, :, 0:NE], 1.0, None, ALU.subtract).then_inc(route_step, 1)
            v.tensor_copy(cnti[:], cntf).then_inc(tables_ready, 1)
            v.wait_ge(route_step, 14)
            v.wait_ge(tables_ready, 1)
            most = v.value_load(cnti[0:1, 0:1], min_val=0, max_val=T)

            def select(e):
                for b in range(TB):
                    i = v.tensor_scalar(S[:, b, :], iota_s[:, 0:CAP], posm[:, b, bass.ds(e, 1)], None, ALU.is_equal)
                i.then_inc(sel_ready, 1)

            def one_hot(which, e, ready):
                v.tensor_scalar(oneh[:, which, :], ident[0:NE, bass.ds(e, 1)].to_broadcast([NE, CAP]), 1.0, None,
                                ALU.mult).then_inc(ready, 1)

            def gathered(g):
                v.wait_ge(gather_done, g + 1)
                v.tensor_tensor(xT, ps[:, 2, :].rearrange("p (c s) -> p c s", c=KC),
                                gains[:, 2, :].unsqueeze(2).to_broadcast([P, KC, CAP]), ALU.mult).then_inc(xt_ready, 1)

            def add_to_residual(n, b):
                v.wait_ge(scatter_done, 2 * n + b + 1)
                v.tensor_tensor(xs[:, b, :], ps[:, 6:8, :].rearrange("p h n -> p (h n)"), xs[:, b, :], ALU.add
                                ).then_inc(added, 1)

            def item(level, e, first):
                n, g = NE * level + e, (NE + 1) * level + e
                if not (first and isinstance(level, int)):
                    v.wait_ge(st_done, n)
                for b in range(TB):
                    i = v.tensor_scalar(SG[:, b, :], iota_s[:], posm[:, b, bass.ds(e, 1)], gtab[:, b, bass.ds(e, 1)],
                                        ALU.is_equal, ALU.mult)
                i.then_inc(sg_ready, 1)
                v.wait_ge(gather_done, g + 1)
                select(e + 1)
                if not first:
                    for b in range(TB):
                        add_to_residual(n - 1, b)
                one_hot(1, e, ohd_ready)
                v.wait_ge(ring_used, 12 * n + KC)
                gu = ps[:, 0:2, :].rearrange("p k (n two) -> p k n two", two=2)
                v.tensor_scalar(gm.rearrange("p (k n) -> p k n", k=2), gu[:, :, :, 0], LIMIT, None, ALU.min
                                ).then_inc(g_clamped, 1)
                v.tensor_scalar(um.rearrange("p (k n) -> p k n", k=2), gu[:, :, :, 1], -LIMIT, LIMIT, ALU.max, ALU.min
                                ).then_inc(u_clamped, 1)
                v.wait_ge(g_clamped, n + 1)
                v.wait_ge(u_clamped, n + 1)
                v.scalar_tensor_tensor(um, um, 1.0, gm, ALU.add, ALU.mult).then_inc(u_times_g, 1)
                v.wait_ge(u_times_g, n + 1)
                v.wait_ge(sig_ready, n + 1)
                v.tensor_tensor(act, um, sg, ALU.mult).then_inc(act_ready, 1)
                gathered(g + 1)
                one_hot(0, e + 1, ohg_ready)

            def experts(level):
                if not isinstance(level, int):
                    v.wait_ge(sg_ready, NE * level)
                    v.wait_ge(sel_ready, (NE + 1) * level)
                    v.tensor_scalar(posm[:], posm[:], float(CAP), None, ALU.subtract).then_inc(shifted, 1)
                    v.wait_ge(shifted, level)
                    v.wait_ge(gather_done, (NE + 1) * level)
                    v.wait_ge(ohg_ready, (NE + 1) * level)
                select(0)
                one_hot(0, 0, ohg_ready)
                gathered((NE + 1) * level)
                item(level, 0, True)
                with v.Fori(1, NE) as e:
                    item(level, e, False)
                for b in range(TB):
                    add_to_residual(NE * level + NE - 1, b)

            v.wait_ge(biases_in, 48)
            experts(0)
            with v.If(most > CAP):
                with v.Fori(1, LEVELS) as level:
                    experts(level)
            v.memset(flag[:], 0.0).then_inc(final_step, 1)
            for b in range(TB):
                normalise(xs, b, 6 + b, xs).then_inc(final_step, 1)
                v.wait_ge(final_step, 2 * b + 2)
                v.tensor_tensor(xs[:, b, :], xs[:, b, :], gfin, ALU.mult).then_inc(final_step, 1)

        @block.tensor
        def _(t):
            mm = t.matmul

            def rows_T(src, task, bank):
                b, half = task // 2 % 2, task % 2
                view = src[:, b, :].rearrange("p (k c) -> p c k", c=KC)
                for c in range(4):
                    i = t.transpose(ps[:, bank, P * c:P * c + P], view[:, 4 * half + c, :], ident[:])
                i.then_inc(xT_done, 1)

            t.wait_ge(masks_ready, 15)
            for k in range(4):
                t.wait_ge(xn_ready, k // 2 + 1)
                rows_T(xrows, k, k)

            def tokens_by(src, name, b, bank, signal):
                w = wcols(name)
                for c in range(KC):
                    i = mm(ps[:, bank, :], src[:, c, P * b:P * b + P], w[:, c, :], start=c == 0, stop=c == KC - 1)
                i.then_inc(signal, 1)

            def split_mm(dst, stationary, moving, start, stop):
                mm(dst, stationary[0], moving[0], start=start, stop=False)
                mm(dst, stationary[0], moving[1], start=False, stop=False)
                return mm(dst, stationary[1], moving[0], start=False, stop=stop)

            def stream_parts(name):
                n = streams[at[name]][3]
                return high_of_stream(at[name], n), low_of_stream(at[name], n)

            def split_tokens_by(src, name, b, bank, signal):
                w = stream_parts(name)
                for c in range(KC):
                    if c % 2 == 0:
                        t.wait_ge(w_low_ready, KC // 2 * at[name] + c // 2 + 1)
                    i = split_mm(ps[:, bank, 0:streams[at[name]][3]], [m[:, c, P * b:P * b + P] for m in src],
                                 [m[:, c, :] for m in w], c == 0, c == KC - 1)
                i.then_inc(signal, 1)

            def release():
                t.nop().then_inc(group_used, 1)

            t.wait_ge(hT_low_ready, 4)
            for b in range(TB):
                split_tokens_by(hT_parts, "q_a", b, b, proj_done)
            t.wait_ge(proj_done, 2)
            release()
            for k in range(4, 8):
                t.wait_ge(xn_ready, 2 + (k - 4) // 2 + 1)
                rows_T(memrows, k, k)
            for b in range(TB):
                split_tokens_by(hT_parts, "kvc_kvs", b, 2 + b, proj_done)
            t.wait_ge(proj_done, 4)
            release()
            for b in range(TB):
                t.wait_ge(rope_step, 4 * (b + 1))
                split_tokens_by(hT_parts, "kvw_gl", b, b, proj_done)
            t.wait_ge(proj_done, 6)
            release()
            for b in range(TB):
                t.wait_ge(rope_step, 4 * (4 + 2 * b))
                t.wait_ge(proj_copied, 2 * (b + 1))
                split_tokens_by(hT_parts, "v_f", b, 2 + b, proj_done)
            t.wait_ge(proj_done, 8)
            release()
            t.wait_ge(consts_in, 16 * 9)
            t.wait_ge(hT_low_ready, 8)
            for b in range(TB):
                for c in range(KC):
                    for k, part in enumerate(hT_parts):
                        i = mm(ps[:, 4, FH * b:FH * b + FH], part[:, c, P * b:P * b + P].bitcast(F32), wfl[:, c, :],
                               start=c == 0 and k == 0, stop=c == KC - 1 and k == 1)
            i.then_inc(proj_done, 1)

            def tile_by(src, name, j, dst):
                w = stream_parts(name)
                for c in range(KC):
                    if c % 2 == 0:
                        t.wait_ge(w_low_ready, KC // 2 * at[name] + c // 2 + 1)
                    i = split_mm(dst, [m[:, c, P * j:P * j + P] for m in w], [m[:, c, :] for m in src],
                                 c == 0, c == KC - 1)
                return i

            def wst(task):
                bank = 4 + task % 4
                kind, half = task // 2, task % 2
                if task >= 4:
                    t.wait_ge(wst_copied, task - 3)
                if task == 0:
                    t.wait_ge(forget_step, 1)
                name = ("m_k", "m_v", "q_f", "k_f", "q_m")[kind]
                if kind == 1:
                    split_tokens_by(mT_parts, name, half, bank, wst_done)
                else:
                    for j in range(2):
                        i = tile_by(mT_parts if kind == 0 else hT_parts, name, 2 * half + j, ps[:, bank, T * j:T * j + T])
                    i.then_inc(wst_done, 1)
                if half == 1:
                    t.wait_ge(wst_done, task + 1)
                    release()

            def branch_tile(m):
                first = MT + (m - MT) // KC * KC
                name, _, row = BRANCH[first]
                j = m - first
                if j == 0:
                    arrived(t, name)
                if m - 2 < MT:
                    t.wait_ge(merge_exp, m - 1)
                else:
                    t.wait_ge(branch_read, m - MT - 1)
                w = group(at[name]).rearrange("p (c n) -> p c n", c=4)
                for c in range(4):
                    i = mm(ps[:, 6 + m % 2, 0:T], w[:, c, P * j:P * j + P], oT[:, row + c, :],
                           start=c == 0, stop=c == 3)
                i.then_inc(branch_done, 1)
                if j == KC - 1:
                    t.wait_ge(branch_done, m - MT + 1)
                    release()

            pieces = iter([("gate", m, half) for m in range(MT) for half in range(2)]
                          + [("branch", m, 0) for m in range(nsa0, fox0)])

            def filler():
                what, m, half = next(pieces)
                if what == "branch":
                    if m == nsa0:
                        t.wait_ge(heads_copied, 4)
                    if m == mem0:
                        t.wait_ge(heads_copied, 8)
                    branch_tile(m)
                    return
                if half == 0:
                    t.wait_ge(tile_low_ready, m + 1)
                    if m >= 2:
                        t.wait_ge(merge_exp, m - 1)
                w = high_of_tile(m), low_of_tile(m)
                for c in range(4 * half, 4 * half + 4):
                    i = split_mm(ps[:, 6 + m % 2, 0:T], [k[:, c, :] for k in w], [k[:, c, :] for k in hT_parts],
                                 c == 0, c == KC - 1)
                if half == 1:
                    i.then_inc(merge_done, 1)
                    if m % 4 == 3:
                        t.wait_ge(merge_done, m + 1)
                        release()

            wst(0)
            t.wait_ge(rope_step, 4 * 8)
            t.wait_ge(proj_copied, 6)
            t.wait_ge(gl_exp, 2)
            for b in range(TB):
                for r in range(REP):
                    i = t.transpose(ps[:, b, P * r:P * r + P], qr[:, b, P * r:P * r + P], ident[:])
                i.then_inc(kqT_done, 1)
            t.wait_ge(proj_copied, 8)
            for b in range(TB):
                for k in range(4):
                    i = t.transpose(ps[:, 2 + b, P * k:P * k + P], kr[:, b, k, :], ident[:])
                i.then_inc(kqT_done, 1)
            for task in (1, 2):
                wst(task)
            t.wait_ge(kqT_ready, 4)
            t.wait_ge(forget_step, 4)
            mm(ps[0:FH, 0, 0:T], logf[:, 0, :], triU[:], start=True, stop=False)
            mm(ps[0:FH, 0, P:T], logf[:, 1, :], triU[:, 0:P], start=False, stop=True)
            mm(ps[:, 1, 0:FH], triU[:, 0:P], logf[:, 0, :], start=True, stop=True)
            mm(ps[:, 1, FH:2 * FH], triU[:, P:T], logf[:, 0, :], start=True, stop=False)
            mm(ps[:, 1, FH:2 * FH], triU[:, 0:P], logf[:, 1, :], start=False, stop=True).then_inc(cum_done, 1)
            for kv in range(2):
                t.transpose(ps[:, 2, CMP * kv:CMP * kv + CMP], pe[:, kv, :], ident[0:CMP, 0:CMP])
            t.transpose(ps[:, 2, 2 * CMP:2 * CMP + MT], bmrow[:], ident[0:MT, 0:MT]).then_inc(peT_done, 1)
            for task in range(3, 10):
                wst(task)
            arrived(t, "w1")
            t.wait_ge(blk_ready, 8)
            t.wait_ge(cum_copied, 2)
            for kv in range(2):
                for l in range(STRIDE):
                    i = mm(z[:, kv, 0:2 * NCMP], w1[:, kv, l, :], blk[:, kv, l, :, :].rearrange("p g n -> p (g n)"),
                           start=l == 0, stop=l == STRIDE - 1)
            i.then_inc(z_done, 1)
            t.wait_ge(z_done, 1)
            release()
            t.wait_ge(wst_copied, 10)
            filler()
            filler()
            t.wait_ge(z_ready, 1)
            for g in range(2):
                mm(ps[HD * g:HD * g + HD, 2, 0:NCMP], w2[:, 0, :], zs[:, 0, g, 0:NCMP], start=True, stop=True)
            for g in range(2):
                for j in range(4):
                    i = mm(ps[32 * j:32 * j + 32, 3, HD * g:HD * g + HD], zs[:, 1, g, :], w2[:, 1, :],
                           start=True, stop=True)
            i.then_inc(cmp_done, 1)
            filler()
            filler()
            t.wait_ge(cmp_ready, 2)
            for b in range(TB):
                for h in range(NH):
                    g, r = h // REP, h % REP
                    half = slice(HD * g, HD * g + HD)
                    col = 16 * (REP * b + r)
                    i = mm(ps[:, g, col:col + NCMP], qT[half, r, P * b:P * b + P], kcmpT[half, 0:NCMP],
                           start=True, stop=True)
            i.then_inc(sc_done, 1)
            for _ in range(4):
                filler()
            t.wait_ge(pc_ready, 1)
            t.wait_ge(peT_ready, 2)
            for q in range(2):
                for b in range(TB):
                    i = t.transpose(ps[:, 2, T * q + P * b:T * q + P * b + P],
                                    pc[:, b, 4 * q:4 * q + 4, :].rearrange("p h n -> p (h n)"), ident[:])
            i.then_inc(pcT_done, 1)
            t.wait_ge(pcT_ready, 1)
            t.wait_ge(cum_rows, 16 * FH)
            t.wait_ge(gl_step, 2)

            def scores(u):
                kind, h = units[u]
                bank = ps[:, u % 2, :]
                if u >= 2:
                    t.wait_ge(exp_done, u - 1)
                if kind == "mem":
                    for b in range(TB):
                        i = mm(bank[:, T * b:T * b + T], qmT[:, h, P * b:P * b + P], kmT[:, h, :],
                               start=True, stop=True)
                    i.then_inc(score_done, 1)
                    return
                if kind == "fox":
                    q, k = qfk[:, 0, h, :], qfk[:, 1, h, :]
                else:
                    half = slice(HD * (h // REP), HD * (h // REP) + HD)
                    q, k = qT[half, h % REP, :], kT[half, 0 if kind == "slc" else 1, :]
                mm(bank[:, 0:P], q[:, 0:P], k[:, 0:P], start=True, stop=False)
                mm(bank[:, 0:P], identb[:], causal[:], start=False, stop=True)
                mm(bank[:, P:3 * P], q[:, P:T], k[:, :], start=True, stop=False)
                mm(bank[:, 2 * P:3 * P], identb[:], causal[:], start=False, stop=True).then_inc(score_done, 1)

            def transposed(u):
                t.wait_ge(prob_ready, u + 1)
                if u >= 2:
                    t.wait_ge(probT_ready, u - 1)
                n = 4 if units[u][0] == "mem" else 3
                src = (0, 2, 1, 3) if n == 4 else (0, 1, 2)
                for k in range(n):
                    i = t.transpose(ps[:, 2 + u % 2, P * k:P * k + P], prob[:, u % 2, P * src[k]:P * src[k] + P],
                                    ident[:])
                i.then_inc(probT_done, 1)

            def values(u):
                kind, h = units[u]
                t.wait_ge(probT_ready, u + 1)
                og = closed[min(c for c in closed if c >= u)]
                bank = ps[:, 4 + og % 2, :]
                pT = probT[:, u % 2, :]
                if og >= 2 and (u - 1) in closed:
                    t.wait_ge(heads_copied, og - 1)
                if kind == "mem":
                    mm(bank[:, 0:T], vm[:, 0, P * h:P * h + P], pT[:, 0:T], start=True, stop=False)
                    i = mm(bank[:, 0:T], vm[:, 1, P * h:P * h + P], pT[:, T:2 * T], start=False, stop=True)
                else:
                    rows = slice(HD * (h % 2), HD * (h % 2) + HD)
                    if kind == "fox":
                        v0, v1 = (vf[:, b, HD * h:HD * h + HD] for b in range(TB))
                    else:
                        g = h // REP
                        v0, v1 = (vsw[:, b, 0 if kind == "slc" else 1, HD * g:HD * g + HD] for b in range(TB))
                    if kind == "slc":
                        quarter = slice(32 * (h % 4), 32 * (h % 4) + NCMP)
                        mm(bank[rows, 0:T], vcmp[quarter, g, :], pcT[quarter, h // 4, :], start=True, stop=False)
                    mm(bank[rows, 0:T], v0, pT[:, 0:T], start=kind == "fox", stop=False)
                    i = mm(bank[rows, P:T], v1, pT[:, T:T + P], start=False, stop=kind != "slc")
                if u in closing:
                    i.then_inc(heads_done, 1)

            for s in range(len(units) + 1):
                if s < len(units):
                    scores(s)
                    filler()
                if s >= 1:
                    transposed(s - 1)
                if s < len(units):
                    filler()
                if s >= 1:
                    values(s - 1)

            t.wait_ge(heads_copied, len(closed))
            for m in range(fox0, fox0 + KC):
                branch_tile(m)
            t.wait_ge(merged_ready, 2 * KC)
            for b in range(TB):
                for half in range(2):
                    arrived(t, f"out{half}")
                    tokens_by(mergedT, f"out{half}", b, 2 * b + half, out_done)
                    if b == TB - 1:
                        t.wait_ge(out_done, TB + half + 1)
                        release()
                        if half == 0:
                            t.wait_ge(xn_ready, 5)
                            rows_T(xn, 8, 4)
                            rows_T(xn, 9, 5)
            t.wait_ge(late_in, 32)
            for b in range(TB):
                if b == 1:
                    t.wait_ge(xn_ready, 6)
                    rows_T(xn, 10, 6)
                    rows_T(xn, 11, 7)
                t.wait_ge(hT_ready, 10 + 2 * b)
                for c in range(KC):
                    i = mm(ps[:, 0, NE * b:NE * b + NE], hT[:, c, P * b:P * b + P], wrout[:, c, :],
                           start=c == 0, stop=c == KC - 1)
            i.then_inc(router_done, 1)
            t.wait_ge(sel_table, 1)
            mm(ps[:, 1, 0:NE], triU[:, 0:P], sel[:, 0, :], start=True, stop=True)
            mm(ps[:, 1, NE:2 * NE], triU[:, P:T], sel[:, 0, :], start=True, stop=False)
            mm(ps[:, 1, NE:2 * NE], triU[:, 0:P], sel[:, 1, :], start=False, stop=True)
            mm(ps[:, 1, 2 * NE:3 * NE], triU[:, P:T], sel[:, 0, :], start=True, stop=False)
            mm(ps[:, 1, 2 * NE:3 * NE], triU[:, P:T], sel[:, 1, :], start=False, stop=True).then_inc(pos_done, 1)
            t.wait_ge(tables_ready, 1)
            most = t.value_load(cnti[0:1, 0:1], min_val=0, max_val=T)

            xview = xn[:, :, :].rearrange("p b (k c) -> p b c k", c=KC)

            def gather(g):
                t.wait_ge(sel_ready, g + 1)
                for c in range(KC):
                    for b in range(TB):
                        i = mm(ps[:, 2, CAP * c:CAP * c + CAP], xview[:, b, c, :], S[:, b, :],
                               start=b == 0, stop=b == TB - 1)
                i.then_inc(gather_done, 1)

            def scatter(b):
                for h in range(2):
                    half = slice(64 * h, 64 * h + 64)
                    i = mm(ps[:, 6 + h, :], ST[half, b, :], oE[half, :], start=True, stop=True)
                i.then_inc(scatter_done, 1)

            def item(level, e, first):
                n, g = NE * level + e, (NE + 1) * level + e
                t.wait_ge(ohg_ready, g + 1)
                t.wait_ge(xt_ready, g + 1)
                for k in range(2):
                    for h in range(2):
                        half = slice(64 * h, 64 * h + 64)
                        mm(ps[half, k, :], oneh[:, 0, :], biases[:, F * h + 512 * k:F * h + 512 * k + 512],
                           start=True, stop=False)
                in_extra = NX if first and isinstance(level, int) else 0
                for c in range(KC):
                    t.wait_ge(slot_full[c], 16 * (n + 1))
                    w = extra if c < in_extra else ring
                    for k in range(2):
                        for h in range(2):
                            half = slice(64 * h, 64 * h + 64)
                            i = mm(ps[half, k, :], xT[:, c, :], w[:, c, F * h + 512 * k:F * h + 512 * k + 512],
                                   start=False, stop=c == KC - 1)
                    i.then_inc(ring_used, 1)
                    if not first and c == 1:
                        t.wait_ge(out_copied, n)
                        t.wait_ge(st_copied, n)
                        scatter(0)
                    if not first and c == 4:
                        t.wait_ge(added, 2 * n - 1)
                        scatter(1)
                gather(g + 1)
                t.wait_ge(sg_ready, n + 1)
                for b in range(TB):
                    i = t.transpose(ps[:, 4, P * b:P * b + P], SG[:, b, :], ident[:])
                i.then_inc(st_done, 1)
                t.wait_ge(act_ready, n + 1)
                view = act.rearrange("p (m r) -> p r m", r=4)
                for r in range(4):
                    i = t.transpose(ps[:, 3, P * r:P * r + P], view[:, r, :], ident[:])
                i.then_inc(actT_done, 1)
                t.wait_ge(ohd_ready, n + 1)
                for h in range(2):
                    half = slice(64 * h, 64 * h + 64)
                    mm(ps[half, 5, :], oneh[:, 1, :], biases[:, 2 * F + 512 * h:2 * F + 512 * h + 512],
                       start=True, stop=False)
                t.wait_ge(actT_copied, n + 1)
                for s in range(4):
                    t.wait_ge(slot_full[KC + s], 16 * (n + 1))
                    for k in range(2):
                        r = 2 * (s % 2) + k
                        lhs = actT[:, P * r + 64 * (s // 2):P * r + 64 * (s // 2) + 64]
                        for h in range(2):
                            half = slice(64 * h, 64 * h + 64)
                            i = mm(ps[half, 5, :], lhs, ring[:, KC + s, 1024 * k + 512 * h:1024 * k + 512 * h + 512],
                                   start=False, stop=s == 3 and k == 1)
                    i.then_inc(ring_used, 1)

            def experts(level):
                if not isinstance(level, int):
                    t.wait_ge(xt_ready, (NE + 1) * level)
                gather((NE + 1) * level)
                item(level, 0, True)
                with t.Fori(1, NE) as e:
                    item(level, e, False)
                last = NE * level + NE - 1
                t.wait_ge(out_copied, last + 1)
                t.wait_ge(st_copied, last + 1)
                scatter(0)
                t.wait_ge(added, 2 * last + 1)
                scatter(1)
                t.wait_ge(added, 2 * last + 2)

            t.wait_ge(biases_in, 48)
            experts(0)
            with t.If(most > CAP):
                with t.Fori(1, LEVELS) as level:
                    experts(level)
            t.wait_ge(final_step, 1)


_INS = ['x', 'mem', 'g_mix', 'w_in', 'b_forget', 'b_merge', 'nsa_pe_k', 'nsa_w1_k', 'nsa_w2_k', 'nsa_pe_v',
        'nsa_w1_v', 'nsa_w2_v', 'g_mem', 'w_mem_kv', 'w_branch_nsa', 'w_branch_fox', 'w_branch_mem', 'w_out',
        'g_ffn', 'w_router', 'b_router', 'w_gate_up', 'b_gate_up', 'w_down', 'b_down', 'g_final']


def _rope_table(np, seq, dim):
    inv = (10000.0 ** (-np.arange(0, dim, 2, dtype=np.float32) / np.float32(dim))).astype(np.float32)
    ang = np.arange(seq, dtype=np.float32)[:, None] * inv[None, :]
    c, s = np.cos(ang), np.sin(ang)
    return np.concatenate([c, c, -s, s], axis=1).astype(np.float32)


def kernel(**inputs):
    import concourse.bacc as _bacc
    import numpy as np
    from concourse.bass_utils import run_bass_kernel_spmd as _run

    arrays = {"in_rope": _rope_table(np, 256, 64)}
    for name in _INS:
        arrays[f"in_{name}"] = np.ascontiguousarray(inputs[name])
    nc = _bacc.Bacc("TRN2", target_bir_lowering=False, num_devices=1)
    args = [nc.dram_tensor(n, a.shape, F32, kind="ExternalInput").ap() for n, a in arrays.items()]
    out = nc.dram_tensor("out_0", arrays["in_x"].shape, F32, kind="ExternalOutput").ap()
    hybrid_layer(nc, *args, out)
    r = _run(nc, [arrays], core_ids=[0])
    return r.results[0]["out_0"]
```

```python
from contextlib import ExitStack

import concourse.bass as bass
from concourse import mybir

F32 = mybir.dt.float32
F32R = mybir.dt.float32r
BF16 = mybir.dt.bfloat16
I32 = mybir.dt.int32
U32 = mybir.dt.uint32
ALU = mybir.AluOpType
ACT = mybir.ActivationFunctionType
AX = mybir.AxisListType.X

P = 128
HD = 64
CAP = 64
NEG = -1e30
EPS = 1e-5
LIMIT = 7.0
ALPHA = 1.702


def hybrid_layer(nc, rope, x, mem, g_mix, w_in, b_forget, b_merge, nsa_pe_k, nsa_w1_k, nsa_w2_k, nsa_pe_v,
                 nsa_w1_v, nsa_w2_v, g_mem, w_mem_kv, w_branch_nsa, w_branch_fox, w_branch_mem, w_out,
                 g_ffn, w_router, b_router, w_gate_up, b_gate_up, w_down, b_down, g_final, out):
    _, T, D = x.shape
    KC = D // P
    TB = T // P
    NE = w_gate_up.shape[1]
    F = w_down.shape[2]
    CMP = nsa_pe_k.shape[1]
    STRIDE = CMP // 2
    NCMP = T // STRIDE - 1
    FH = b_forget.shape[1]
    NH = FH
    REP = NH // 2
    MH = w_branch_mem.shape[1] // P
    MT = 3 * D // P
    LEVELS = T // CAP
    SCALE = HD ** -0.5
    MSCALE = P ** -0.5
    assert T == 256 and D == 1024 and NE == 32 and F == D and MH == 4 and NH == 8

    Q_A, K_C, K_W, GL, Q_F, K_F, V_F, F_L, Q_M, MERGE = 0, 512, 1024, 1280, 1304, 1816, 2328, 2840, 2848, 3360

    with ExitStack() as ctx:
        address = {}

        def sb(name, shape, dt=F32):
            address[name] = (nc.sbuf_base + 31) // 32 * 32
            return ctx.enter_context(nc.sbuf_tensor(name, shape, dt))

        def rounded(name, over, first, shape):
            return nc.alloc_sbuf_tensor_at(name, shape, F32R, offset=address[over] + 4 * first)

        def sem(name):
            return ctx.enter_context(nc.semaphore(name))

        ps = ctx.enter_context(nc.psum_tensor("ps", [P, 8, 512], F32))

        ring = sb("ring", [P, 12, 2048])
        NG = 4
        gates = ring[:, 8:11, :].rearrange("p s n -> p (s n)").rearrange("p (m t) -> p m t", t=T)

        def group(i):
            pos = (i + 3) % NG
            return ring[:, 2 * pos:2 * pos + 2, :].rearrange("p s n -> p (s n)")

        ring_high = rounded("ring_high", "ring", 8 * 2048, [P, 4 * 2048])
        out_high = rounded("out_high", "ring", 0, [P, 2, 2 * 2048])
        ring_low = rounded("ring_low", "ring", 0, [P, 8 * 2048])

        def high_of_stream(i, n):
            if i >= at["out0"]:
                return out_high[:, i - at["out0"], :].rearrange("p (c n) -> p c n", c=KC)
            return ring_high[:, 4096 * (i % 2):4096 * (i % 2) + KC * n].rearrange("p (c n) -> p c n", c=KC)

        def low_of_stream(i, n=512):
            pos = (i + 3) % NG
            return ring_low[:, 4096 * pos:4096 * pos + KC * n].rearrange("p (c n) -> p c n", c=KC)

        def high_of_tile(m):
            first = 3 * 2048 + 1024 * (m % 2)
            return ring_high[:, first:first + 1024].rearrange("p (c n) -> p c n", c=KC)

        xs = sb("xs", [P, TB, D])
        xn = sb("xn", [P, TB, D])
        hT = sb("hT", [P, KC, T])
        hT_parts = hT_high, _ = rounded("hT_high", "xn", 0, [P, KC, T]), rounded("hT_low", "hT", 0, [P, KC, T])
        mT = sb("mT", [P, KC, T])
        mergedT = mT
        ident = sb("ident", [P, P])
        identb = sb("identb", [P, P], BF16)
        causal = sb("causal", [P, P], BF16)
        cneg = sb("cneg", [P, TB, 1, 16])
        cone = sb("cone", [P, TB, 1, 16])
        triU = sb("triU", [P, T])
        iota_e = sb("iota_e", [P, NE])
        iota_s = sb("iota_s", [P, P])
        rp = sb("rp", [P, TB, 2, HD])
        gains = sb("gains", [P, 3, KC])
        bmrow = sb("bmrow", [MT, P])
        bmerge = sb("bmerge", [P, MT])
        eps = sb("eps", [P, 1])
        flag = sb("flag", [P, 1])
        stats = sb("stats", [P, 3, 8])
        bforget = sb("bforget", [P, 1, FH])
        brouter = sb("brouter", [P, 1, NE])
        wrout = sb("wrout", [P, KC, NE])
        w2 = sb("w2", [HD, 2, HD])
        pe = sb("pe", [CMP, 2, P])
        peT = sb("peT", [P, 2, CMP])

        early = sb("early", [P, 3072])
        qr = early[:, 0:1024].rearrange("p (b n) -> p b n", b=TB)
        kr = early[:, 1024:2048].rearrange("p (b k n) -> p b k n", b=TB, k=4)
        blk = early[:, 2048:3008].rearrange("p (k l g n) -> p k l g n", k=2, l=STRIDE, g=2)
        merged_high = [rounded(f"merged_high{k}", "early", 2048 * k, [P, KC // 2, T]) for k in range(2)]
        oT = early[:, 0:3072].rearrange("p (j t) -> p j t", t=T)
        NX = 4
        extra = sb("extra", [P, NX, 2048])
        space = extra[:, :, :].rearrange("p s n -> p (s n)")
        qfk = space[0:HD + 1, 0:4096].rearrange("p (a h t) -> p a h t", a=2, h=FH)
        qmT = space[:, 4096:5120].rearrange("p (h t) -> p h t", h=MH)
        kmT = space[:, 5120:6144].rearrange("p (h t) -> p h t", h=MH)
        kT = space[:, 6144:7168].rearrange("p (k t) -> p k t", k=4)
        vf = space[:, 7168:8192].rearrange("p (b n) -> p b n", b=TB)
        xrows = space[:, 4096:6144].rearrange("p (b n) -> p b n", b=TB)
        memrows = space[:, 6144:8192].rearrange("p (b n) -> p b n", b=TB)
        mT_parts = mT_high, _ = rounded("mT_high", "extra", 2048, [P, KC, T]), rounded("mT_low", "mT", 0, [P, KC, T])
        attn = sb("attn", [P, 3584])
        vm = attn[:, 0:1024].rearrange("p (b n) -> p b n", b=TB)
        vsw = attn[:, 1024:1536].rearrange("p (b k n) -> p b k n", b=TB, k=2)
        ropet = attn[:, 1536:2560].rearrange("p (a n) -> p a n", a=2)
        glg = sb("glg", [P, TB, 24])
        fz = sb("fz", [P, 4, TB, FH])
        logf = sb("logf", [P, TB, FH])
        cumT = sb("cumT", [FH, T])
        cumtok = sb("cumtok", [P, TB, FH])
        qT = sb("qT", [P, REP, T])
        zt = sb("zt", [HD, 3, 2, 32])
        zs = sb("zs", [HD, 2, 2, 32])
        kcmpT = sb("kcmpT", [P, 16])
        vcmp = sb("vcmp", [P, 2, HD])
        cst = sb("cst", [P, 3, TB, NH, 1])
        pc = sb("pc", [P, TB, NH, 32])
        pcT = sb("pcT", [P, 2, T])
        prob = ropet
        probT = attn[:, 2560:3584].rearrange("p (a n) -> p a n", a=2)
        sc = probT[:, :, 0:TB * NH * 16].rearrange("p k (b h n) -> p k b h n", b=TB, h=NH)
        UN = 28
        st_mx = sb("st_mx", [P, UN, 2])
        st_mf = sb("st_mf", [P, UN, 2])
        st_nb = sb("st_nb", [P, UN, 2])
        st_sum = sb("st_sum", [P, UN, 2])
        st_cl = sb("st_cl", [P, UN, 2])
        st_rc = sb("st_rc", [P, UN, 2])
        st_rg = sb("st_rg", [P, UN, 2])

        late = {"used": 0}
        late_space = qT[:, :, :].rearrange("p r t -> p (r t)")

        def reused(*shape):
            n = 1
            for d in shape:
                n *= d
            flat = late_space[:, late["used"]:late["used"] + n]
            late["used"] += n
            if len(shape) == 1:
                return flat
            return flat.rearrange("p (a b) -> p a b", a=shape[0])

        lg = reused(TB, NE)
        m8 = reused(TB, 8)
        i8 = reused(TB, 8).bitcast(U32)
        idxf = reused(TB, 8)
        nm = reused(TB)
        e4 = reused(TB, 4)
        s4 = reused(TB)
        r4 = reused(TB)
        eq, eqg = (early[:, 1024 + 256 * k:1280 + 256 * k].rearrange("p (b j e) -> p b j e", b=TB, j=4) for k in range(2))
        sel = reused(TB, NE)
        cntf = reused(1)
        posm = sb("posm", [P, TB, NE + 1])
        gtab = sb("gtab", [P, TB, NE + 1])
        cnti = sb("cnti", [P, 1], I32)

        biases = attn[0:NE, 0:3 * F]
        gfin = mT[:, 4:8, :].rearrange("p c t -> p (c t)")
        xT = mT[:, 0:2, :].rearrange("p c t -> p (c t)").rearrange("p (c s) -> p c s", c=KC)
        S = reused(TB, CAP)
        SG = reused(TB, P)
        ST = reused(TB, P)
        oneh = reused(2, CAP)[0:NE]
        gm = early[:, 0:512]
        um = early[:, 512:1024]
        sg = early[:, 1024:1536]
        act = early[:, 1536:2048]
        actT = early[:, 2048:2560]
        oE = early[:, 2560:3072]

        x_in = [sem(f"x_in{b}") for b in range(TB)]
        mem_in, forget_in, rope_in, bforget_in, small_in, consts_in, late_in, biases_in = (sem(n) for n in (
            "mem_in", "forget_in", "rope_in", "bforget_in", "small_in", "consts_in", "late_in", "biases_in"))
        first_in = [sem(f"first_in{k}") for k in range(KC // 2)]
        group_full = [sem(f"group_full{i}") for i in range(NG)]
        group_used = sem("group_used")
        masks_ready, masks_step = sem("masks_ready"), sem("masks_step")
        eps_set, squares, roots, recips, xn_ready = sem("eps_set"), sem("squares"), sem("roots"), sem("recips"), sem("xn_ready")
        xT_done, hT_ready, hT_high_ready, hT_low_ready = (sem(n) for n in (
            "xT_done", "hT_ready", "hT_high_ready", "hT_low_ready"))
        w_high_ready, w_low_ready = sem("w_high_ready"), sem("w_low_ready")
        tile_high_ready, tile_low_ready = sem("tile_high_ready"), sem("tile_low_ready")
        proj_done, rope_done, proj_copied = sem("proj_done"), sem("rope_done"), sem("proj_copied")
        rope_step = sem("rope_step")
        kqT_done, kqT_ready = sem("kqT_done"), sem("kqT_ready")
        wst_done, wst_copied = sem("wst_done"), sem("wst_copied")
        forget_step, forget_act = sem("forget_step"), sem("forget_act")
        cum_done, cum_copied, cum_rows = sem("cum_done"), sem("cum_copied"), sem("cum_rows")
        peT_done, peT_ready, blk_ready = sem("peT_done"), sem("peT_ready"), sem("blk_ready")
        z_done, z_exp, z_step, z_ready = sem("z_done"), sem("z_exp"), sem("z_step"), sem("z_ready")
        cmp_done, cmp_ready = sem("cmp_done"), sem("cmp_ready")
        gl_exp, gl_step = sem("gl_exp"), sem("gl_step")
        sc_done, sc_step, sc_exp, pc_ready, pcT_done, pcT_ready = (sem(n) for n in (
            "sc_done", "sc_step", "sc_exp", "pc_ready", "pcT_done", "pcT_ready"))
        score_done, max_done, bias_step, bias_ready, exp_done = (sem(n) for n in (
            "score_done", "max_done", "bias_step", "bias_ready", "exp_done"))
        norm_step, prob_ready, probT_done, probT_ready = (sem(n) for n in (
            "norm_step", "prob_ready", "probT_done", "probT_ready"))
        heads_done, heads_copied = sem("heads_done"), sem("heads_copied")
        merge_done, merge_tanh, gate_ready = sem("merge_done"), sem("merge_tanh"), sem("gate_ready")
        branch_done, branch_read, merged_ready = sem("branch_done"), sem("branch_read"), sem("merged_ready")
        merged_high_ready, merged_low_ready = sem("merged_high_ready"), sem("merged_low_ready")
        out_done, x2_ready = sem("out_done"), sem("x2_ready")
        router_done, route_step, route_exp, sel_table = (sem(n) for n in (
            "router_done", "route_step", "route_exp", "sel_table"))
        pos_done, tables_ready = sem("pos_done"), sem("tables_ready")
        slot_full = [sem(f"slot_full{i}") for i in range(12)]
        ring_used = sem("ring_used")
        sel_ready, gather_done, xt_ready, sg_ready = (sem(n) for n in (
            "sel_ready", "gather_done", "xt_ready", "sg_ready"))
        ohg_ready, ohd_ready = sem("ohg_ready"), sem("ohd_ready")
        st_done, st_copied, g_clamped, u_clamped, u_times_g = (sem(n) for n in (
            "st_done", "st_copied", "g_clamped", "u_clamped", "u_times_g"))
        sig_ready, act_ready, actT_done, actT_copied = (sem(n) for n in (
            "sig_ready", "act_ready", "actT_done", "actT_copied"))
        out_copied, scatter_done, added = (sem(n) for n in (
            "out_copied", "scatter_done", "added"))
        shifted = sem("shifted")
        gain_in = sem("gain_in")
        final_step, stored = sem("final_step"), sem("stored")

        def w_rows(w, c0, n):
            return w[0].rearrange("(p c) n -> p c n", c=KC)[:, :, c0:c0 + n]

        def w_chunks(w, k0, n0, n):
            return w[0].rearrange("(c p) n -> p c n", p=P)[:, :, n0:n0 + n]

        streams = ([("q_a", w_in, Q_A, 512), ("kvc_kvs", w_in, K_C, 512), ("kvw_gl_fl", w_in, K_W, 280 + FH),
                    ("v_f", w_in, V_F, 512), ("m_k", w_mem_kv, 0, 512), ("m_v", w_mem_kv, 512, 512),
                    ("q_f", w_in, Q_F, 512), ("k_f", w_in, K_F, 512), ("q_m", w_in, Q_M, 512),
                    ("w1", None, 0, 0)]
                   + [(f"merge{i}", w_in, MERGE + 512 * i, 512) for i in range(6)]
                   + [("b_nsa", w_branch_nsa, 0, 0), ("b_mem", w_branch_mem, 0, 0), ("b_fox", w_branch_fox, 0, 0),
                      ("out0", w_out, 0, 512), ("out1", w_out, 512, 512)])
        at = {name: i for i, (name, _, _, _) in enumerate(streams)}
        NS = len(streams)

        def wcols(name, n=512):
            return group(at[name])[:, 0:KC * n].rearrange("p (c n) -> p c n", c=KC)

        def arrived(eng, name):
            i = at[name]
            eng.wait_ge(group_full[i % NG], sum(64 if streams[j][0] == "w1" else 16 for j in range(i, 0, -NG)))

        def first_piece(i):
            return KC // 2 * (i if i < at["w1"] else at["w1"] + i - at["out0"])

        def pieces_of(i):
            n = streams[i][3]
            for k in range(KC // 2):
                yield (first_piece(i) + k, *(w[:, 2 * k:2 * k + 2, :] for w in (
                    wcols(streams[i][0], n), high_of_stream(i, n), low_of_stream(i, n))))

        def merge_cols(m):
            return wcols(f"merge{m // 4}")[:, :, P * (m % 4):P * (m % 4) + P]

        def low_of_tile(m):
            return low_of_stream(at[f"merge{m // 4}"])[:, :, P * (m % 4):P * (m % 4) + P]

        w1 = group(at["w1"])[:, 0:2 * STRIDE * HD].rearrange("p (k l e) -> p k l e", k=2, l=STRIDE)

        z = ps[0:HD, 0, 0:64].rearrange("p (k c) -> p k c", k=2)

        first_places = [extra[:, s, :] for s in range(NX)] + [ring[:, s, :] for s in range(NX, 12)]
        second_places = ([ring[:, s, :] for s in range(NX)] + [extra[:, s, :] for s in range(NX)]
                         + [hT[:, :, :].rearrange("p c t -> p (c t)")] + [ring[:, s, :] for s in range(4, 7)])
        third_places = [ring[:, (s + 7) % 12, :] for s in range(9)] + [extra[:, s, :] for s in range(3)]
        places_of_all = [ring[:, (s + 7) % 12, :] for s in range(12)]

        block = ctx.enter_context(nc.Block())

        units = ([("slc" if br == 0 else "win", h) for h in range(NH) for br in range(2)]
                 + [("mem", h) for h in range(MH)] + [("fox", h) for h in range(FH)])
        PRE = 4
        nsa0, mem0, fox0 = MT, MT + KC, MT + 2 * KC
        BRANCH = {nsa0: ("b_nsa", 0, 0), mem0: ("b_mem", 2, 8), fox0: ("b_fox", 1, 4)}

        def tiles_ending(s):
            last = 2 * (MT - PRE) // 2
            return [PRE + s] if s < last else [nsa0 + 2 * (s - last) + k for k in range(2)] if s < len(units) else []

        def nsa_gate(kind, h):
            return glg[:, :, 3 * h + {"cmp": 0, "slc": 1, "win": 2}[kind]]

        closing = {u: (u // 4 if k in ("slc", "win") else 4 + h // 2 if k == "fox" else 8 + h)
                   for u, (k, h) in enumerate(units)
                   if (k == "win" and h % 2) or (k == "fox" and h % 2) or k == "mem"}
        closed = {}
        for u in sorted(closing):
            closed[u] = len(closed)

        @block.sync
        def _(sp):
            for b in range(TB):
                sp.dma_start(xs[:, b, :], x[0, P * b:P * b + P, :]).then_inc(x_in[b], 16)
            for i, (name, w, c0, n) in enumerate(streams):
                if i == 0:
                    for g, w_g in enumerate((g_mix, g_mem, g_ffn)):
                        sp.dma_start(gains[:, g, :], w_g[0].rearrange("(p c) -> p c", c=KC)).then_inc(small_in, 16)
                    for k in range(KC // 2):
                        two = slice(2 * k, 2 * k + 2)
                        sp.dma_start(wcols(name)[:, two, :], w_rows(w, c0, n)[:, two, :]).then_inc(first_in[k], 16)
                    continue
                if i == 1:
                    sp.dma_start(memrows, mem[0].rearrange("(b p) n -> p b n", p=P)).then_inc(mem_in, 16)
                if i == 2:
                    sp.dma_start(wcols(name, n)[:, :, 280:n], w_rows(w_in, F_L, FH)).then_inc(forget_in, 16)
                    sp.dma_start(rp[:], rope.rearrange("(b p) (k n) -> p b k n", p=P, k=2)).then_inc(rope_in, 16)
                if i == 3:
                    sp.dma_start(bforget[:, 0, :], b_forget[0].partition_broadcast(P)).then_inc(bforget_in, 16)
                if i == NG:
                    sp.dma_start(bmrow[:], b_merge[0].rearrange("(m p) -> m p", p=P)).then_inc(consts_in, 16)
                    for kv, (wk, pk) in enumerate(((nsa_w2_k, nsa_pe_k), (nsa_w2_v, nsa_pe_v))):
                        sp.dma_start(w2[:, kv, :], wk[0]).then_inc(consts_in, 16)
                        for half in range(2):
                            sp.dma_start(pe[:, kv, HD * half:HD * half + HD], pk[0]).then_inc(consts_in, 16)
                    sp.dma_start(wrout[:], w_rows(w_router, 0, NE)).then_inc(late_in, 16)
                    sp.dma_start(brouter[:, 0, :], b_router[0].partition_broadcast(P)).then_inc(late_in, 16)
                if name == "merge1":
                    sp.wait_ge(cum_copied, 1)
                    for h in range(FH):
                        sp.dma_start(qfk[HD:HD + 1, 1, h, :], cumT[h:h + 1, :]).then_inc(cum_rows, 16)
                if i >= NG:
                    sp.wait_ge(group_used, i - NG + 1)
                full = group_full[i % NG]
                if name == "w1":
                    for half in range(2):
                        for kv, wk in enumerate((nsa_w1_k, nsa_w1_v)):
                            sp.dma_start(w1[HD * half:HD * half + HD, kv],
                                         wk[0, STRIDE * half:STRIDE * half + STRIDE].rearrange("l d e -> d l e")
                                         ).then_inc(full, 16)
                elif name[0:2] == "b_":
                    sp.dma_start(group(i).rearrange("p (c n) -> p c n", c=4),
                                 w[0].rearrange("(c p) n -> p c n", p=P)).then_inc(full, 16)
                elif name[0:3] == "out":
                    sp.dma_start(wcols(name), w[0].rearrange("(c p) n -> p c n", p=P)[:, :, c0:c0 + n]
                                 ).then_inc(full, 16)
                else:
                    cols = min(n, 280) if i == 2 else n
                    sp.dma_start(wcols(name, n)[:, :, 0:cols], w_rows(w, c0, cols)).then_inc(full, 16)

            def slot_load(s, e, places):
                if s < KC:
                    src = w_gate_up[0, bass.ds(e, 1)].rearrange("a (p c) n -> (a p) c n", c=KC)[:, s, :]
                else:
                    h, q = (s - KC) // 2, (s - KC) % 2
                    src = w_down[0, bass.ds(e, 1)].rearrange("a (h m r) n -> (a m) h (r n)", h=2, r=4
                                                              )[:, h, 2048 * q:2048 * q + 2048]
                sp.dma_start(places[s], src).then_inc(slot_full[s], 16)

            sp.wait_ge(heads_done, len(closed))
            for s in range(NX):
                slot_load(s, 0, first_places)
            sp.wait_ge(merged_ready, 2 * KC)
            for s in range(KC, 12):
                slot_load(s, 0, first_places)
            for s in range(NX, KC):
                sp.wait_ge(group_used, NS - NG + s // 2 + 1)
                slot_load(s, 0, first_places)
            for s in (*range(NX), KC, *range(NX, KC), *range(KC + 1, 12)):
                if s == KC:
                    sp.wait_ge(router_done, 1)
                elif s >= NX:
                    sp.wait_ge(ring_used, s - NX + (s < KC))
                sp.wait_ge(slot_full[s], 16)
                slot_load(s, 1, second_places)
            for s in range(12):
                sp.wait_ge(ring_used, s + 8)
                sp.wait_ge(slot_full[s], 32)
                slot_load(s, 2, third_places)

            def item(level, e):
                for s in range(12):
                    sp.wait_ge(ring_used, 12 * (NE * level + e - 1) + s + 1)
                    slot_load(s, e, places_of_all)

            with sp.Fori(3, NE) as e:
                item(0, e)
            sp.wait_ge(tables_ready, 1)
            most = sp.value_load(cnti[0:1, 0:1], min_val=0, max_val=T)
            with sp.If(most > CAP):
                with sp.Fori(1, LEVELS) as level:
                    with sp.Fori(0, NE) as e:
                        item(level, e)
            for b in range(TB):
                sp.wait_ge(final_step, b + 2)
                sp.dma_start(out[0, P * b:P * b + P, :], xs[:, b, :]).then_inc(stored, 16)
            sp.wait_ge(stored, 16 * TB)

        @block.gpsimd
        def _(pool):
            pool.memset(ident[:], 0.0).then_inc(masks_step, 1)
            pool.memset(identb[:], 0.0).then_inc(masks_step, 1)
            pool.memset(causal[:], 0.0).then_inc(masks_step, 1)
            pool.memset(cneg[:], 0.0).then_inc(masks_step, 1)
            pool.memset(cone[:], 1.0).then_inc(masks_step, 1)
            pool.memset(triU[:], 1.0).then_inc(masks_step, 1)
            pool.wait_ge(masks_step, 6)
            for m in (ident, identb):
                pool.affine_select(out=m[:], in_=m[:], compare_op=ALU.not_equal, fill=1.0, base=0,
                                   pattern=[[-1, P]], channel_multiplier=1).then_inc(masks_ready, 1)
            pool.memset(zs[:], 0.0).then_inc(masks_ready, 1)
            pool.memset(pc[:], 0.0).then_inc(masks_ready, 1)
            pool.wait_ge(masks_ready, 4)
            pool.memset(qfk[HD:HD + 1, 0], 1.0).then_inc(masks_ready, 1)
            pool.wait_ge(masks_ready, 5)
            pool.affine_select(out=causal[:], in_=causal[:], compare_op=ALU.is_ge, fill=NEG, base=0,
                               pattern=[[-1, P]], channel_multiplier=1).then_inc(masks_ready, 1)
            for b in range(TB):
                for m, fill in ((cneg, NEG), (cone, 0.0)):
                    pool.affine_select(out=m[:, b, 0, :], in_=m[:, b, 0, :], compare_op=ALU.is_ge, fill=fill,
                                       base=P * b - (CMP - 1), pattern=[[-STRIDE, 16]], channel_multiplier=1
                                       ).then_inc(masks_ready, 1)
            pool.affine_select(out=triU[:, 0:P], in_=triU[:, 0:P], compare_op=ALU.is_ge, fill=0.0, base=0,
                               pattern=[[1, P]], channel_multiplier=-1).then_inc(masks_ready, 1)
            pool.iota(iota_e[:], pattern=[[1, NE]], base=0, channel_multiplier=0,
                      allow_small_or_imprecise_dtypes=True).then_inc(masks_ready, 1)
            pool.iota(iota_s[:], pattern=[[0, 2], [1, CAP]], base=0, channel_multiplier=0,
                      allow_small_or_imprecise_dtypes=True).then_inc(masks_ready, 1)
            pool.memset(posm[:], -1.0).then_inc(masks_ready, 1)
            pool.memset(gtab[:], 0.0).then_inc(masks_ready, 1)

        @block.scalar
        def _(a):
            scr = early[:, D:2 * D]

            def square_root_of(src, b, k):
                a.activation(scr, src[:, b, :], ACT.Square, accum_out=stats[:, 0, k:k + 1]).then_inc(squares, 1)
                a.wait_ge(squares, k + 1)
                a.activation(stats[:, 1, k:k + 1], stats[:, 0, k:k + 1], ACT.Sqrt, scale=1.0 / D, bias=eps[:, 0:1]
                             ).then_inc(roots, 1)

            def high_of(i):
                arrived(a, streams[i][0])
                if streams[i][0] == "kvw_gl_fl":
                    a.wait_ge(forget_in, 16)
                if i >= 2:
                    a.wait_ge(group_used, i - 1)
                for _, raw, high, _ in pieces_of(i):
                    a.activation(high, raw, ACT.Copy).then_inc(w_high_ready, 1)

            def high_of_hT(src, dst, task):
                b, half = task // 2 % 2, task % 2
                part = (slice(None), slice(4 * half, 4 * half + 4), slice(P * b, P * b + P))
                a.wait_ge(hT_ready, task + 1)
                a.activation(dst[part], src[part], ACT.Copy).then_inc(hT_high_ready, 1)

            a.wait_ge(eps_set, 1)
            for b in range(TB):
                a.wait_ge(x_in[b], 16)
                square_root_of(xs, b, b)
            for k, (_, raw, high, _) in enumerate(pieces_of(0)):
                a.wait_ge(first_in[k], 16)
                a.activation(high, raw, ACT.Copy).then_inc(w_high_ready, 1)
                if k < 2:
                    high_of_hT(hT, hT_high, k)
            for t in range(2, 4):
                high_of_hT(hT, hT_high, t)
            a.wait_ge(mem_in, 16)
            for b in range(TB):
                square_root_of(memrows, b, 2 + b)
            high_of(1)
            high_of(2)
            for t in range(4, 8):
                high_of_hT(mT, mT_high, t)

            for b in range(TB):
                a.wait_ge(proj_done, 3 + b)
                a.activation(kr[:, b, 3, :], ps[:, 2 + b, 128:256], ACT.Copy).then_inc(proj_copied, 1)
                a.activation(vsw[:, b, 0, :], ps[:, 2 + b, 384:512], ACT.Copy).then_inc(proj_copied, 1)
            high_of(3)
            for b in range(TB):
                a.wait_ge(proj_done, 5 + b)
                a.activation(vsw[:, b, 1, :], ps[:, b, 128:256], ACT.Copy).then_inc(proj_copied, 1)
                a.activation(glg[:, b, :], ps[:, b, 256:280], ACT.Exp, scale=-1.0).then_inc(gl_exp, 1)
            high_of(4)
            for b in range(TB):
                a.wait_ge(proj_done, 7 + b)
                a.activation(vf[:, b, :], ps[:, 2 + b, :], ACT.Copy).then_inc(proj_copied, 1)
            high_of(5)
            for b in range(TB):
                a.wait_ge(kqT_done, 1 + b)
                a.activation(qT[:, :, P * b:P * b + P], ps[:, b, :].rearrange("p (r t) -> p r t", r=REP), ACT.Copy
                             ).then_inc(kqT_ready, 1)
            for b in range(TB):
                a.wait_ge(kqT_done, 3 + b)
                a.activation(kT[:, :, P * b:P * b + P], ps[:, 2 + b, :].rearrange("p (k t) -> p k t", k=4), ACT.Copy
                             ).then_inc(kqT_ready, 1)
            a.wait_ge(forget_step, 3)
            a.activation(fz[:, 2], fz[:, 1], ACT.Exp, scale=-1.0).then_inc(forget_act, 1)
            a.wait_ge(forget_act, 1)
            a.activation(fz[:, 3], fz[:, 2], ACT.Ln, bias=1.0).then_inc(forget_act, 1)

            def high_of_merge(m):
                if m % 4 == 0:
                    arrived(a, f"merge{m // 4}")
                if m >= 2:
                    a.wait_ge(merge_done, m - 1)
                a.activation(high_of_tile(m), merge_cols(m), ACT.Copy).then_inc(tile_high_ready, 1)

            for t in range(10):
                a.wait_ge(wst_done, t + 1)
                bank = ps[:, 4 + t % 4, :]
                pair = bank.rearrange("p (j t) -> p j t", j=2)
                kind, half = t // 2, t % 2
                if kind == 0:
                    a.activation(kmT[:, 2 * half:2 * half + 2, :], pair, ACT.Copy).then_inc(wst_copied, 1)
                elif kind == 1:
                    a.activation(vm[:, half, :], bank, ACT.Copy).then_inc(wst_copied, 1)
                elif kind == 4:
                    a.activation(qmT[:, 2 * half:2 * half + 2, :], pair, ACT.Copy).then_inc(wst_copied, 1)
                else:
                    for odd in range(2):
                        heads = qfk[0:HD, kind - 2, 4 * half + odd:4 * half + odd + 3:2, :]
                        i = a.activation(heads, pair[HD * odd:HD * odd + HD], ACT.Copy)
                    i.then_inc(wst_copied, 1)
                if t == 3:
                    a.wait_ge(cum_done, 1)
                    a.activation(cumT[:], ps[0:FH, 0, 0:T], ACT.Copy, scale=-1.0 / SCALE).then_inc(cum_copied, 1)
                    a.activation(cumtok[:], ps[:, 1, 0:TB * FH].rearrange("p (b h) -> p b h", b=TB), ACT.Copy
                                 ).then_inc(cum_copied, 1)
                    a.wait_ge(peT_done, 1)
                    a.activation(peT[:], ps[:, 2, 0:2 * CMP].rearrange("p (k l) -> p k l", k=2), ACT.Copy
                                 ).then_inc(peT_ready, 1)
                    a.activation(bmerge[:], ps[:, 2, 2 * CMP:2 * CMP + MT], ACT.Copy, scale=0.5
                                 ).then_inc(peT_ready, 1)
                if t in (1, 3, 5):
                    high_of(6 + t // 2)
                if t == 7:
                    a.wait_ge(group_used, at["k_f"] + 1)
                    high_of_merge(0)
                    high_of_merge(1)

            def gate_tanh(m):
                a.wait_ge(merge_done, m + 1)
                a.activation(gates[:, m, :], ps[:, 6 + m % 2, 0:T], ACT.Tanh, scale=0.5, bias=bmerge[:, m:m + 1]
                             ).then_inc(merge_tanh, 1)
                if m + 2 < MT:
                    high_of_merge(m + 2)

            a.wait_ge(peT_ready, 2)
            a.wait_ge(z_done, 1)
            a.activation(zt[:, 0, :, 0:2 * NCMP], z[:, :, 0:2 * NCMP], ACT.Exp, scale=-1.0).then_inc(z_exp, 1)
            gate_tanh(0)
            a.wait_ge(cmp_done, 1)
            a.activation(kcmpT[:, 0:NCMP], ps[:, 2, 0:NCMP], ACT.Copy).then_inc(cmp_ready, 1)
            a.activation(vcmp[:], ps[:, 3, 0:2 * HD].rearrange("p (g d) -> p g d", g=2), ACT.Copy
                         ).then_inc(cmp_ready, 1)
            gate_tanh(1)
            a.wait_ge(sc_step, 3)
            a.activation(sc[:, 1, :, :, 0:NCMP], sc[:, 0, :, :, 0:NCMP], ACT.Exp, scale=SCALE).then_inc(sc_exp, 1)
            gate_tanh(2)
            gate_tanh(3)
            a.wait_ge(pcT_done, 1)
            a.activation(pcT[:], ps[:, 2, :].rearrange("p (q t) -> p q t", q=2), ACT.Copy).then_inc(pcT_ready, 1)

            for s in range(len(units) + 1):
                if s < len(units):
                    kind, h = units[s]
                    a.wait_ge(bias_ready, s + 1)
                    if s >= 2:
                        a.wait_ge(probT_done, s - 1)
                    bank = ps[:, s % 2, :]
                    scale = MSCALE if kind == "mem" else SCALE
                    cols = ((0, 256), (256, 512)) if kind == "mem" else ((0, 128), (128, 384))
                    for q, (c0, c1) in enumerate(cols):
                        i = a.activation(prob[:, s % 2, c0:c1], bank[:, c0:c1], ACT.Exp, scale=scale,
                                         bias=st_nb[:, s, q:q + 1], accum_out=st_sum[:, s, q:q + 1])
                    i.then_inc(exp_done, 1)
                if s >= 1:
                    a.wait_ge(probT_done, s)
                    n = 512 if units[s - 1][0] == "mem" else 384
                    a.activation(probT[:, (s - 1) % 2, 0:n], ps[:, 2 + (s - 1) % 2, 0:n], ACT.Copy
                                 ).then_inc(probT_ready, 1)
                for m in tiles_ending(s):
                    if m < MT:
                        gate_tanh(m)
                for u in ([s - 2] if s < len(units) else [s - 2, s - 1]):
                    if u in closing:
                        a.wait_ge(heads_done, closed[u] + 1)
                        a.activation(oT[:, closing[u], :], ps[:, 4 + closed[u] % 2, 0:T], ACT.Copy
                                     ).then_inc(heads_copied, 1)
            a.wait_ge(group_used, at["b_mem"] + 1)
            for half in range(2):
                arrived(a, f"out{half}")
                for _, raw, high, _ in pieces_of(at[f"out{half}"]):
                    a.activation(high, raw, ACT.Copy).then_inc(w_high_ready, 1)
                if half == 0:
                    for q in range(KC // 2):
                        a.wait_ge(merged_ready, KC + 2 * q + 2)
                        a.activation(merged_high[q // 2][:, 2 * (q % 2):2 * (q % 2) + 2, :],
                                     mergedT[:, 2 * q:2 * q + 2, :], ACT.Copy).then_inc(merged_high_ready, 1)
                    a.wait_ge(group_used, at["b_fox"] + 1)

            a.wait_ge(heads_done, len(closed))
            a.dma_start(biases[:, 0:2 * F], b_gate_up[0]).then_inc(biases_in, 16)
            a.dma_start(biases[:, 2 * F:3 * F], b_down[0]).then_inc(biases_in, 16)

            for b in range(TB):
                a.wait_ge(x2_ready, 3 + b)
                square_root_of(xs, b, 4 + b)
            a.wait_ge(out_done, 2 * TB)
            a.dma_start(gfin, g_final.partition_broadcast(P)).then_inc(gain_in, 16)
            a.wait_ge(route_step, 5)
            for b in range(TB):
                a.activation(e4[:, b, :], m8[:, b, 0:4], ACT.Exp, bias=nm[:, b:b + 1], accum_out=s4[:, b:b + 1]
                             ).then_inc(route_exp, 1)

            def item(level, e):
                n = NE * level + e
                a.wait_ge(g_clamped, n + 1)
                a.activation(sg, gm, ACT.Sigmoid, scale=ALPHA).then_inc(sig_ready, 1)
                a.wait_ge(st_done, n + 1)
                a.activation(ST, ps[:, 4, 0:TB * P].rearrange("p (b t) -> p b t", b=TB), ACT.Copy
                             ).then_inc(st_copied, 1)
                a.wait_ge(actT_done, n + 1)
                a.activation(actT, ps[:, 3, :], ACT.Copy).then_inc(actT_copied, 1)
                a.wait_ge(ring_used, 12 * n + 12)
                a.activation(oE, ps[:, 5, :], ACT.Copy).then_inc(out_copied, 1)

            a.wait_ge(tables_ready, 1)
            most = a.value_load(cnti[0:1, 0:1], min_val=0, max_val=T)
            with a.Fori(0, NE) as e:
                item(0, e)
            with a.If(most > CAP):
                with a.Fori(1, LEVELS) as level:
                    with a.Fori(0, NE) as e:
                        item(level, e)
            for b in range(TB):
                a.wait_ge(final_step, 1)
                square_root_of(xs, b, 6 + b)

        @block.vector
        def _(v):
            v.memset(eps[:], EPS).then_inc(eps_set, 1)

            def normalise(src, b, k, dst):
                v.wait_ge(roots, k + 1)
                v.reciprocal(stats[:, 2, k:k + 1], stats[:, 1, k:k + 1]).then_inc(recips, 1)
                v.wait_ge(recips, k + 1)
                return v.tensor_scalar(dst[:, b, :], src[:, b, :], stats[:, 2, k:k + 1], None, ALU.mult)

            for b in range(TB):
                normalise(xs, b, b, xrows).then_inc(xn_ready, 1)
            v.wait_ge(masks_ready, 15)

            def to_hT(dst, g, task, bank):
                b, half = task // 2 % 2, task % 2
                v.wait_ge(xT_done, task + 1)
                v.tensor_tensor(dst[:, 4 * half:4 * half + 4, P * b:P * b + P],
                                ps[:, bank, :].rearrange("p (c t) -> p c t", c=4),
                                gains[:, g, 4 * half:4 * half + 4].unsqueeze(2).to_broadcast([P, 4, P]), ALU.mult
                                ).then_inc(hT_ready, 1)

            def low_of_hT(parts, raw, task):
                b, half = task // 2 % 2, task % 2
                high, low, raw = (m[:, 4 * half:4 * half + 4, P * b:P * b + P] for m in (*parts, raw))
                v.wait_ge(hT_high_ready, task + 1)
                v.tensor_tensor(low, raw, high.bitcast(F32), ALU.subtract).then_inc(hT_low_ready, 1)

            def low_of_piece(n, raw, high, low):
                v.wait_ge(w_high_ready, n + 1)
                v.tensor_tensor(low, raw, high.bitcast(F32), ALU.subtract).then_inc(w_low_ready, 1)

            def low_of(i):
                for piece in pieces_of(i):
                    low_of_piece(*piece)

            first_pieces = list(pieces_of(0))

            def low_of_merge(m):
                v.wait_ge(tile_high_ready, m + 1)
                v.tensor_tensor(low_of_tile(m), merge_cols(m), high_of_tile(m).bitcast(F32), ALU.subtract
                                ).then_inc(tile_low_ready, 1)

            v.wait_ge(small_in, 48)
            for t in range(2):
                to_hT(hT, 0, t, t)
            for t in range(2):
                low_of_hT(hT_parts, hT, t)
                low_of_piece(*first_pieces[t])
            for t in range(2, 4):
                to_hT(hT, 0, t, t)
            for t in range(2, 4):
                low_of_piece(*first_pieces[t])
            for t in range(2, 4):
                low_of_hT(hT_parts, hT, t)
            for b in range(TB):
                normalise(memrows, b, 2 + b, memrows).then_inc(xn_ready, 1)
            low_of(1)

            nrope = [0]

            def roped(src, dst, b, n):
                t0 = ropet[:, 0, 0:n * HD].rearrange("p (h d) -> p h d", h=n)
                t1 = ropet[:, 1, 0:n * HD].rearrange("p (h d) -> p h d", h=n)
                hf = HD // 2
                cos = rp[:, b, 0:1, :].to_broadcast([P, n, HD])
                if nrope[0]:
                    v.wait_ge(rope_step, 4 * nrope[0])
                v.tensor_tensor(t0, src, cos, ALU.mult).then_inc(rope_step, 1)
                v.tensor_tensor(t1[:, :, 0:hf], src[:, :, hf:HD],
                                rp[:, b, 1:2, 0:hf].to_broadcast([P, n, hf]), ALU.mult).then_inc(rope_step, 1)
                v.tensor_tensor(t1[:, :, hf:HD], src[:, :, 0:hf],
                                rp[:, b, 1:2, hf:HD].to_broadcast([P, n, hf]), ALU.mult).then_inc(rope_step, 1)
                v.wait_ge(rope_step, 4 * nrope[0] + 3)
                if n == NH:
                    t0, t1 = (m.rearrange("p (g r) d -> p g r d", g=2) for m in (t0, t1))
                v.tensor_tensor(dst, t0, t1, ALU.add).then_inc(rope_step, 1)
                nrope[0] += 1

            def heads_of(ap, n):
                return ap.rearrange("p (h d) -> p h d", h=n)

            v.wait_ge(rope_in, 16)
            v.wait_ge(squares, 4)
            for b in range(TB):
                v.wait_ge(proj_done, 1 + b)
                roped(heads_of(ps[:, b, :], NH), qr[:, b, :].rearrange("p (r g d) -> p g r d", r=REP, g=2), b, NH)
            for t in range(4, 8):
                to_hT(mT, 1, t, t)
            low_of(2)
            for t in range(4, 8):
                low_of_hT(mT_parts, mT, t)
            for b in range(TB):
                v.wait_ge(proj_copied, 2 * (b + 1))
                roped(heads_of(ps[:, 2 + b, 0:128], 2), heads_of(kr[:, b, 2, :], 2), b, 2)
                roped(heads_of(ps[:, 2 + b, 256:384], 2), heads_of(kr[:, b, 0, :], 2), b, 2)
            low_of(3)
            for b in range(TB):
                v.wait_ge(gl_exp, 1 + b)
                roped(heads_of(ps[:, b, 0:128], 2), heads_of(kr[:, b, 1, :], 2), b, 2)
            v.wait_ge(bforget_in, 16)
            v.tensor_tensor(fz[:, 0], ps[:, 0:TB, 280:280 + FH],
                            bforget[:].to_broadcast([P, TB, FH]), ALU.add).then_inc(forget_step, 1)
            low_of(4)
            v.wait_ge(forget_step, 1)
            v.tensor_scalar(fz[:, 2], fz[:, 0], -1.0, None, ALU.mult).then_inc(forget_step, 1)
            v.wait_ge(forget_step, 2)
            v.tensor_tensor(fz[:, 1], fz[:, 0], fz[:, 2], ALU.max).then_inc(forget_step, 1)
            low_of(5)
            v.wait_ge(gl_exp, 2)
            v.tensor_scalar(glg[:], glg[:], 1.0, None, ALU.add).then_inc(gl_step, 1)
            v.wait_ge(gl_step, 1)
            v.reciprocal(glg[:], glg[:]).then_inc(gl_step, 1)
            v.wait_ge(forget_act, 2)
            v.scalar_tensor_tensor(logf[:], fz[:, 0], 0.0, fz[:, 3], ALU.min, ALU.subtract).then_inc(forget_step, 1)
            def gate_of_tile(m):
                v.wait_ge(merge_tanh, m + 1)
                v.tensor_scalar(gates[:, m, :], gates[:, m, :], 0.5, 0.5, ALU.mult, ALU.add).then_inc(gate_ready, 1)

            def branch_of_tile(m):
                k, j = (m - MT) // KC, (m - MT) % KC
                gate = gates[:, KC * (0, 2, 1)[k] + j, :]
                v.wait_ge(branch_done, m - MT + 1)
                if k == 0:
                    v.wait_ge(gate_ready, MT)
                    v.tensor_tensor(mergedT[:, j, :], ps[:, 6 + m % 2, 0:T], gate, ALU.mult).then_inc(branch_read, 1)
                    return
                v.tensor_tensor(gate, ps[:, 6 + m % 2, 0:T], gate, ALU.mult).then_inc(branch_read, 1)
                v.wait_ge(branch_read, m - MT + 1)
                v.tensor_tensor(mergedT[:, j, :], mergedT[:, j, :], gate, ALU.add).then_inc(merged_ready, 1)
                v.wait_ge(merged_ready, m - MT - KC + 1)

            low_of(6)
            v.wait_ge(peT_ready, 1)
            v.wait_ge(kqT_ready, 4)
            for kv in range(2):
                for half in range(2):
                    for g in range(2):
                        rows = slice(HD * g, HD * g + HD)
                        places = slice(STRIDE * half, STRIDE * half + STRIDE)
                        src = kT[rows, 2 + kv, STRIDE * half:STRIDE * half + STRIDE * NCMP]
                        v.tensor_tensor(blk[HD * half:HD * half + HD, kv, :, g, :],
                                        src.rearrange("p (n l) -> p l n", l=STRIDE),
                                        peT[rows, kv, places].unsqueeze(2).to_broadcast([HD, STRIDE, NCMP]), ALU.add
                                        ).then_inc(blk_ready, 1)
            low_of(7)
            low_of(8)
            low_of_merge(0)
            low_of_merge(1)
            v.wait_ge(z_exp, 1)
            v.tensor_scalar(zt[:, 1, :, 0:2 * NCMP], zt[:, 0, :, 0:2 * NCMP], 1.0, None, ALU.add).then_inc(z_step, 1)
            v.wait_ge(z_step, 1)
            v.reciprocal(zt[:, 2, :, 0:2 * NCMP], zt[:, 1, :, 0:2 * NCMP]).then_inc(z_step, 1)
            v.wait_ge(z_step, 2)
            for kv in range(2):
                i = v.tensor_tensor(zs[:, kv, :, 0:NCMP], z[:, kv, 0:2 * NCMP].rearrange("p (g n) -> p g n", g=2),
                                    zt[:, 2, kv, 0:2 * NCMP].rearrange("p (g n) -> p g n", g=2), ALU.mult)
            i.then_inc(z_ready, 1)
            gate_of_tile(0)
            low_of_merge(2)
            gate_of_tile(1)
            low_of_merge(3)
            v.wait_ge(sc_done, 1)
            scm, sce = sc[:, 0, :, :, 0:NCMP], sc[:, 1, :, :, 0:NCMP]
            wide = [P, TB, NH, NCMP]
            for g in range(2):
                raw = ps[:, g, 0:TB * REP * 16].rearrange("p (b r n) -> p b r n", b=TB, r=REP)[:, :, :, 0:NCMP]
                i = v.tensor_tensor(scm[:, :, REP * g:REP * g + REP, :], raw,
                                    cneg[:, :, :, 0:NCMP].to_broadcast([P, TB, REP, NCMP]), ALU.add)
            i.then_inc(sc_step, 1)
            v.wait_ge(sc_step, 1)
            v.tensor_reduce(cst[:, 0], scm, AX, ALU.max).then_inc(sc_step, 1)
            v.wait_ge(sc_step, 2)
            v.tensor_tensor(scm, scm, cst[:, 0].to_broadcast(wide), ALU.subtract).then_inc(sc_step, 1)
            v.wait_ge(sc_exp, 1)
            v.tensor_tensor(sce, sce, cone[:, :, :, 0:NCMP].to_broadcast(wide), ALU.mult).then_inc(sc_step, 1)
            v.wait_ge(sc_step, 4)
            v.tensor_reduce(cst[:, 1], sce, AX, ALU.add).then_inc(sc_step, 1)
            v.wait_ge(sc_step, 5)
            v.tensor_scalar(cst[:, 1], cst[:, 1], 1e-30, None, ALU.max).then_inc(sc_step, 1)
            v.wait_ge(sc_step, 6)
            v.reciprocal(cst[:, 2], cst[:, 1]).then_inc(sc_step, 1)
            v.wait_ge(sc_step, 7)
            v.tensor_tensor(cst[:, 1, :, :, 0], cst[:, 2, :, :, 0],
                            glg[:].rearrange("p b (h k) -> p b h k", k=3)[:, :, :, 0], ALU.mult).then_inc(sc_step, 1)
            v.wait_ge(sc_step, 8)
            v.tensor_tensor(pc[:, :, :, 0:NCMP], sce, cst[:, 1].to_broadcast(wide), ALU.mult).then_inc(pc_ready, 1)
            gate_of_tile(2)
            low_of_merge(4)

            nstep = [0, 0]
            nmax = 0
            v.wait_ge(cum_copied, 2)
            for s in range(len(units) + 1):
                if s < len(units):
                    kind, h = units[s]
                    v.wait_ge(score_done, s + 1)
                    bank = ps[:, s % 2, :]
                    if kind == "mem":
                        v.tensor_reduce(st_mx[:, s, :], bank.rearrange("p (q k) -> p q k", q=2), AX, ALU.max
                                        ).then_inc(max_done, 1)
                        nmax += 1
                    else:
                        v.reduce_max(st_mx[:, s, 0:1], bank[:, 0:128], AX).then_inc(max_done, 1)
                        v.reduce_max(st_mx[:, s, 1:2], bank[:, 128:384], AX).then_inc(max_done, 1)
                        nmax += 2
                    v.wait_ge(max_done, nmax)
                    if kind == "fox":
                        v.scalar_tensor_tensor(st_mf[:, s, :], st_mx[:, s, :], SCALE, cumtok[:, :, h],
                                               ALU.mult, ALU.add).then_inc(bias_step, 1)
                        nstep[0] += 1
                        v.wait_ge(bias_step, nstep[0])
                        v.tensor_tensor(st_nb[:, s, :], cumtok[:, :, h], st_mf[:, s, :], ALU.subtract
                                        ).then_inc(bias_ready, 1)
                    else:
                        v.tensor_scalar(st_nb[:, s, :], st_mx[:, s, :], -(MSCALE if kind == "mem" else SCALE), None,
                                        ALU.mult).then_inc(bias_ready, 1)
                tile = tiles_ending(s - 1)[-1] if s else PRE - 1
                if tile >= MT:
                    branch_of_tile(tile)
                if PRE + s + 1 < MT:
                    low_of_merge(PRE + s + 1)
                if s < len(units):
                    u = s
                    kind, h = units[u]
                    v.wait_ge(exp_done, u + 1)
                    total = st_sum[:, u, :]
                    if kind != "mem":
                        v.tensor_scalar(st_cl[:, u, :], total, 1e-30, None, ALU.max).then_inc(norm_step, 1)
                        nstep[1] += 1
                        v.wait_ge(norm_step, nstep[1])
                        total = st_cl[:, u, :]
                    v.reciprocal(st_rc[:, u, :], total).then_inc(norm_step, 1)
                    nstep[1] += 1
                    v.wait_ge(norm_step, nstep[1])
                    factor = st_rc
                    if kind in ("slc", "win"):
                        v.tensor_tensor(st_rg[:, u, :], st_rc[:, u, :], nsa_gate(kind, h), ALU.mult
                                        ).then_inc(norm_step, 1)
                        nstep[1] += 1
                        v.wait_ge(norm_step, nstep[1])
                        factor = st_rg
                    cols = ((0, 256), (256, 512)) if kind == "mem" else ((0, 128), (128, 384))
                    for q, (c0, c1) in enumerate(cols):
                        i = v.tensor_scalar(prob[:, u % 2, c0:c1], prob[:, u % 2, c0:c1], factor[:, u, q:q + 1], None,
                                            ALU.mult)
                    i.then_inc(prob_ready, 1)
                    if tile < MT:
                        gate_of_tile(tile)
                    if len(tiles_ending(s)) == 2:
                        branch_of_tile(tiles_ending(s)[0])

            def fox_pair(q):
                two = slice(2 * q, 2 * q + 2)
                gate = gates[:, KC + 2 * q:KC + 2 * q + 2, :]
                v.wait_ge(branch_done, 2 * KC + 2 * q + 2)
                v.tensor_tensor(gate, ps[:, 6 + q % 2, :].rearrange("p (j t) -> p j t", j=2), gate, ALU.mult
                                ).then_inc(branch_read, 2)
                v.wait_ge(branch_read, 2 * KC + 2 * q + 2)
                v.tensor_tensor(mergedT[:, two, :], mergedT[:, two, :], gate, ALU.add).then_inc(merged_ready, 2)

            def low_of_merged(q):
                high = merged_high[q // 2][:, 2 * (q % 2):2 * (q % 2) + 2, :]
                two = slice(2 * q, 2 * q + 2)
                v.wait_ge(merged_high_ready, q + 1)
                v.tensor_tensor(mT_parts[1][:, two, :], mergedT[:, two, :], high.bitcast(F32), ALU.subtract
                                ).then_inc(merged_low_ready, 1)

            out_pieces = list(pieces_of(at["out0"]))
            for k in range(2):
                low_of_piece(*out_pieces[k])
            for q in range(KC // 2):
                fox_pair(q)
                if q < 2:
                    low_of_piece(*out_pieces[2 + q])
                low_of_merged(q)
            low_of(at["out1"])
            for task in range(4):
                half, b = task // 2, task % 2
                v.wait_ge(out_done, task + 1)
                cols = slice(512 * half, 512 * half + 512)
                v.tensor_tensor(xs[:, b, cols], ps[:, 2 * b + half, :], xs[:, b, cols], ALU.add).then_inc(x2_ready, 1)
                if task == 2:
                    normalise(xs, 0, 4, xn).then_inc(xn_ready, 1)
                    for t in range(8, 10):
                        to_hT(hT, 2, t, t - 4)
            for t in range(10, 12):
                to_hT(hT, 2, t, t - 4)
            normalise(xs, 1, 5, xn).then_inc(xn_ready, 1)

            v.wait_ge(late_in, 32)
            v.wait_ge(router_done, 1)
            for b in range(TB):
                i = v.scalar_tensor_tensor(lg[:, b, :], ps[:, 0, NE * b:NE * b + NE], stats[:, 2, 4 + b:5 + b],
                                           brouter[:, 0, :], ALU.mult, ALU.add)
            i.then_inc(route_step, 1)
            v.wait_ge(route_step, 1)
            for b in range(TB):
                v.max(m8[:, b, :], lg[:, b, :]).then_inc(route_step, 1)
            v.wait_ge(route_step, 3)
            v.tensor_scalar(nm, m8[:, :, 0], -1.0, None, ALU.mult).then_inc(route_step, 1)
            for b in range(TB):
                i = v.max_index(i8[:, b, :], m8[:, b, :], lg[:, b, :])
            i.then_inc(route_step, 1)
            v.wait_ge(route_step, 5)
            v.tensor_copy(idxf, i8).then_inc(route_step, 1)
            v.wait_ge(route_step, 6)
            four = [P, TB, 4, NE]
            for b in range(TB):
                i = v.tensor_tensor(eq[:, b], iota_e[:].unsqueeze(1).to_broadcast([P, 4, NE]),
                                    idxf[:, b, 0:4].unsqueeze(2).to_broadcast([P, 4, NE]), ALU.is_equal)
            i.then_inc(route_step, 1)
            v.wait_ge(route_step, 7)
            v.tensor_reduce(sel, eq.rearrange("p b j e -> p b e j"), AX, ALU.add).then_inc(sel_table, 1)
            v.wait_ge(pos_done, 1)
            v.tensor_tensor(posm[:, :, 0:NE], ps[:, 1, 0:TB * NE].rearrange("p (b e) -> p b e", b=TB), sel, ALU.mult
                            ).then_inc(route_step, 1)
            v.reduce_max(cntf, ps[:, 1, TB * NE:(TB + 1) * NE], AX).then_inc(route_step, 1)
            v.wait_ge(route_step, 9)
            v.tensor_scalar(posm[:, :, 0:NE], posm[:, :, 0:NE], 1.0, None, ALU.subtract).then_inc(route_step, 1)
            v.tensor_copy(cnti[:], cntf).then_inc(tables_ready, 1)
            v.wait_ge(route_step, 10)
            v.wait_ge(tables_ready, 1)
            most = v.value_load(cnti[0:1, 0:1], min_val=0, max_val=T)

            def select(e):
                for b in range(TB):
                    i = v.tensor_scalar(S[:, b, :], iota_s[:, 0:CAP], posm[:, b, bass.ds(e, 1)], None, ALU.is_equal)
                i.then_inc(sel_ready, 1)

            def one_hot(which, e, ready):
                v.tensor_scalar(oneh[:, which, :], ident[0:NE, bass.ds(e, 1)].to_broadcast([NE, CAP]), 1.0, None,
                                ALU.mult).then_inc(ready, 1)

            def gathered(g):
                v.wait_ge(gather_done, g + 1)
                v.tensor_tensor(xT, ps[:, 2, :].rearrange("p (c s) -> p c s", c=KC),
                                gains[:, 2, :].unsqueeze(2).to_broadcast([P, KC, CAP]), ALU.mult).then_inc(xt_ready, 1)

            def add_to_residual(n, b, bank=6):
                v.wait_ge(scatter_done, 2 * n + b + 1)
                v.tensor_tensor(xs[:, b, :], ps[:, bank:bank + 2, :].rearrange("p h n -> p (h n)"), xs[:, b, :], ALU.add
                                ).then_inc(added, 1)

            def item(level, e, first):
                n, g = NE * level + e, (NE + 1) * level + e
                if not (first and isinstance(level, int)):
                    v.wait_ge(st_done, n)
                for b in range(TB):
                    i = v.tensor_scalar(SG[:, b, :], iota_s[:], posm[:, b, bass.ds(e, 1)], gtab[:, b, bass.ds(e, 1)],
                                        ALU.is_equal, ALU.mult)
                i.then_inc(sg_ready, 1)
                v.wait_ge(gather_done, g + 1)
                select(e + 1)
                if not first:
                    for b in range(TB):
                        add_to_residual(n - 1, b)
                one_hot(1, e, ohd_ready)
                v.wait_ge(ring_used, 12 * n + KC)
                gu = ps[:, 0:2, :].rearrange("p k (n two) -> p k n two", two=2)
                v.tensor_scalar(gm.rearrange("p (k n) -> p k n", k=2), gu[:, :, :, 0], LIMIT, None, ALU.min
                                ).then_inc(g_clamped, 1)
                v.tensor_scalar(um.rearrange("p (k n) -> p k n", k=2), gu[:, :, :, 1], -LIMIT, LIMIT, ALU.max, ALU.min
                                ).then_inc(u_clamped, 1)
                v.wait_ge(g_clamped, n + 1)
                v.wait_ge(u_clamped, n + 1)
                v.scalar_tensor_tensor(um, um, 1.0, gm, ALU.add, ALU.mult).then_inc(u_times_g, 1)
                v.wait_ge(u_times_g, n + 1)
                v.wait_ge(sig_ready, n + 1)
                v.tensor_tensor(act, um, sg, ALU.mult).then_inc(act_ready, 1)
                gathered(g + 1)
                one_hot(0, e + 1, ohg_ready)

            def experts(level):
                if not isinstance(level, int):
                    v.wait_ge(sg_ready, NE * level)
                    v.wait_ge(sel_ready, (NE + 1) * level)
                    v.tensor_scalar(posm[:], posm[:], float(CAP), None, ALU.subtract).then_inc(shifted, 1)
                    v.wait_ge(shifted, level)
                    v.wait_ge(gather_done, (NE + 1) * level)
                    v.wait_ge(ohg_ready, (NE + 1) * level)
                    select(0)
                    one_hot(0, 0, ohg_ready)
                gathered((NE + 1) * level)
                item(level, 0, True)
                with v.Fori(1, NE) as e:
                    item(level, e, False)
                for b, bank in enumerate((6, 0)):
                    add_to_residual(NE * level + NE - 1, b, bank)

            select(0)
            one_hot(0, 0, ohg_ready)
            v.wait_ge(route_exp, 2)
            v.reciprocal(r4, s4).then_inc(route_step, 1)
            v.wait_ge(route_step, 11)
            v.tensor_tensor(e4, e4, r4.unsqueeze(2).to_broadcast([P, TB, 4]), ALU.mult
                            ).then_inc(route_step, 1)
            v.wait_ge(route_step, 12)
            for b in range(TB):
                i = v.tensor_tensor(eqg[:, b], eq[:, b], e4[:, b, :].unsqueeze(2).to_broadcast([P, 4, NE]), ALU.mult)
            i.then_inc(route_step, 1)
            v.wait_ge(route_step, 13)
            v.tensor_reduce(gtab[:, :, 0:NE], eqg.rearrange("p b j e -> p b e j"), AX, ALU.add
                            ).then_inc(route_step, 1)
            v.wait_ge(route_step, 14)

            v.wait_ge(biases_in, 32)
            experts(0)
            with v.If(most > CAP):
                with v.Fori(1, LEVELS) as level:
                    experts(level)
            v.wait_ge(gain_in, 16)
            v.memset(flag[:], 0.0).then_inc(final_step, 1)
            for b in range(TB):
                v.wait_ge(roots, 7 + b)
                v.reciprocal(stats[:, 2, 6 + b:7 + b], stats[:, 1, 6 + b:7 + b]).then_inc(recips, 1)
                v.wait_ge(recips, 7 + b)
                v.scalar_tensor_tensor(xs[:, b, :], xs[:, b, :], stats[:, 2, 6 + b:7 + b], gfin, ALU.mult, ALU.mult
                                       ).then_inc(final_step, 1)

        @block.tensor
        def _(t):
            mm = t.matmul

            def rows_T(src, task, bank):
                b, half = task // 2 % 2, task % 2
                view = src[:, b, :].rearrange("p (k c) -> p c k", c=KC)
                for c in range(4):
                    i = t.transpose(ps[:, bank, P * c:P * c + P], view[:, 4 * half + c, :], ident[:])
                i.then_inc(xT_done, 1)

            t.wait_ge(masks_ready, 15)
            for k in range(4):
                t.wait_ge(xn_ready, k // 2 + 1)
                rows_T(xrows, k, k)

            def split_mm(dst, stationary, moving, start, stop):
                mm(dst, stationary[0], moving[0], start=start, stop=False)
                mm(dst, stationary[0], moving[1], start=False, stop=False)
                return mm(dst, stationary[1], moving[0], start=False, stop=stop)

            def stream_parts(name):
                n = streams[at[name]][3]
                return high_of_stream(at[name], n), low_of_stream(at[name], n)

            def split_tokens_by(src, name, b, bank, signal):
                w = stream_parts(name)
                for c in range(KC):
                    if c % 2 == 0:
                        t.wait_ge(w_low_ready, first_piece(at[name]) + c // 2 + 1)
                    if name == "q_a" and b == 0 and c == 4:
                        t.wait_ge(hT_low_ready, 2)
                    i = split_mm(ps[:, bank, 0:streams[at[name]][3]], [m[:, c, P * b:P * b + P] for m in src],
                                 [m[:, c, :] for m in w], c == 0, c == KC - 1)
                i.then_inc(signal, 1)

            def release():
                t.nop().then_inc(group_used, 1)

            for b in range(TB):
                t.wait_ge(hT_low_ready, 1 if b == 0 else 4)
                split_tokens_by(hT_parts, "q_a", b, b, proj_done)
            t.wait_ge(proj_done, 2)
            release()
            for k in range(4, 8):
                t.wait_ge(xn_ready, 2 + (k - 4) // 2 + 1)
                rows_T(memrows, k, k)
            for b in range(TB):
                split_tokens_by(hT_parts, "kvc_kvs", b, 2 + b, proj_done)
            t.wait_ge(proj_done, 4)
            release()
            for b in range(TB):
                t.wait_ge(rope_step, 4 * (b + 1))
                split_tokens_by(hT_parts, "kvw_gl_fl", b, b, proj_done)
            t.wait_ge(proj_done, 6)
            release()
            for b in range(TB):
                t.wait_ge(rope_step, 4 * (4 + 2 * b))
                t.wait_ge(proj_copied, 2 * (b + 1))
                split_tokens_by(hT_parts, "v_f", b, 2 + b, proj_done)
            t.wait_ge(proj_done, 8)
            release()
            def tile_by(src, name, j, dst):
                w = stream_parts(name)
                for c in range(KC):
                    if c % 2 == 0:
                        t.wait_ge(w_low_ready, first_piece(at[name]) + c // 2 + 1)
                    i = split_mm(dst, [m[:, c, P * j:P * j + P] for m in w], [m[:, c, :] for m in src],
                                 c == 0, c == KC - 1)
                return i

            def wst(task):
                bank = 4 + task % 4
                kind, half = task // 2, task % 2
                if task >= 4:
                    t.wait_ge(wst_copied, task - 3)
                if task == 0:
                    t.wait_ge(hT_low_ready, 8)
                name = ("m_k", "m_v", "q_f", "k_f", "q_m")[kind]
                if kind == 1:
                    split_tokens_by(mT_parts, name, half, bank, wst_done)
                else:
                    for j in range(2):
                        i = tile_by(mT_parts if kind == 0 else hT_parts, name, 2 * half + j, ps[:, bank, T * j:T * j + T])
                    i.then_inc(wst_done, 1)
                if half == 1:
                    t.wait_ge(wst_done, task + 1)
                    release()

            def branch_tile(m):
                first = MT + (m - MT) // KC * KC
                name, _, row = BRANCH[first]
                j = m - first
                if j == 0:
                    arrived(t, name)
                bank = ps[:, 6 + m % 2, 0:T]
                if m >= fox0:
                    bank = ps[:, 6 + j // 2 % 2, T * (j % 2):T * (j % 2) + T]
                    t.wait_ge(branch_read, 2 * KC if j < 4 else 2 * KC + j // 2 * 2 - 2)
                elif m - 2 < MT:
                    t.wait_ge(merge_tanh, m - 1)
                else:
                    t.wait_ge(branch_read, m - MT - 1)
                w = group(at[name]).rearrange("p (c n) -> p c n", c=4)
                for c in range(4):
                    i = mm(bank, w[:, c, P * j:P * j + P], oT[:, row + c, :],
                           start=c == 0, stop=c == 3)
                i.then_inc(branch_done, 1)
                if j == KC - 1:
                    t.wait_ge(branch_done, m - MT + 1)
                    release()

            pieces = iter([("gate", m, half) for m in range(MT) for half in range(2)]
                          + [("branch", m, 0) for m in range(nsa0, fox0)])

            def filler():
                what, m, half = next(pieces)
                if what == "branch":
                    if m == nsa0:
                        t.wait_ge(heads_copied, 4)
                    if m == mem0:
                        t.wait_ge(heads_copied, 8)
                    branch_tile(m)
                    return
                if half == 0:
                    t.wait_ge(tile_low_ready, m + 1)
                    if m >= 2:
                        t.wait_ge(merge_tanh, m - 1)
                w = high_of_tile(m), low_of_tile(m)
                for c in range(4 * half, 4 * half + 4):
                    i = split_mm(ps[:, 6 + m % 2, 0:T], [k[:, c, :] for k in w], [k[:, c, :] for k in hT_parts],
                                 c == 0, c == KC - 1)
                if half == 1:
                    i.then_inc(merge_done, 1)
                    if m % 4 == 3:
                        t.wait_ge(merge_done, m + 1)
                        release()

            wst(0)
            t.wait_ge(rope_step, 4 * 8)
            t.wait_ge(proj_copied, 6)
            t.wait_ge(gl_exp, 2)
            t.wait_ge(forget_step, 1)
            for b in range(TB):
                for r in range(REP):
                    i = t.transpose(ps[:, b, P * r:P * r + P], qr[:, b, P * r:P * r + P], ident[:])
                i.then_inc(kqT_done, 1)
            t.wait_ge(proj_copied, 8)
            for b in range(TB):
                for k in range(4):
                    i = t.transpose(ps[:, 2 + b, P * k:P * k + P], kr[:, b, k, :], ident[:])
                i.then_inc(kqT_done, 1)
            for task in (1, 2):
                wst(task)
            t.wait_ge(kqT_ready, 4)
            t.wait_ge(forget_step, 4)
            mm(ps[0:FH, 0, 0:T], logf[:, 0, :], triU[:], start=True, stop=False)
            mm(ps[0:FH, 0, P:T], logf[:, 1, :], triU[:, 0:P], start=False, stop=True)
            mm(ps[:, 1, 0:FH], triU[:, 0:P], logf[:, 0, :], start=True, stop=True)
            mm(ps[:, 1, FH:2 * FH], triU[:, P:T], logf[:, 0, :], start=True, stop=False)
            mm(ps[:, 1, FH:2 * FH], triU[:, 0:P], logf[:, 1, :], start=False, stop=True).then_inc(cum_done, 1)
            t.wait_ge(consts_in, 16 * 7)
            for kv in range(2):
                t.transpose(ps[:, 2, CMP * kv:CMP * kv + CMP], pe[:, kv, :], ident[0:CMP, 0:CMP])
            t.transpose(ps[:, 2, 2 * CMP:2 * CMP + MT], bmrow[:], ident[0:MT, 0:MT]).then_inc(peT_done, 1)
            for task in range(3, 10):
                wst(task)
            arrived(t, "w1")
            t.wait_ge(blk_ready, 8)
            t.wait_ge(cum_copied, 2)
            for kv in range(2):
                for l in range(STRIDE):
                    i = mm(z[:, kv, 0:2 * NCMP], w1[:, kv, l, :], blk[:, kv, l, :, :].rearrange("p g n -> p (g n)"),
                           start=l == 0, stop=l == STRIDE - 1)
            i.then_inc(z_done, 1)
            t.wait_ge(z_done, 1)
            release()
            t.wait_ge(wst_copied, 10)
            filler()
            filler()
            t.wait_ge(z_ready, 1)
            for g in range(2):
                mm(ps[HD * g:HD * g + HD, 2, 0:NCMP], w2[:, 0, :], zs[:, 0, g, 0:NCMP], start=True, stop=True)
            for g in range(2):
                for j in range(4):
                    i = mm(ps[32 * j:32 * j + 32, 3, HD * g:HD * g + HD], zs[:, 1, g, :], w2[:, 1, :],
                           start=True, stop=True)
            i.then_inc(cmp_done, 1)
            filler()
            filler()
            t.wait_ge(cmp_ready, 2)
            for b in range(TB):
                for h in range(NH):
                    g, r = h // REP, h % REP
                    half = slice(HD * g, HD * g + HD)
                    col = 16 * (REP * b + r)
                    i = mm(ps[:, g, col:col + NCMP], qT[half, r, P * b:P * b + P], kcmpT[half, 0:NCMP],
                           start=True, stop=True)
            i.then_inc(sc_done, 1)
            for _ in range(4):
                filler()
            t.wait_ge(pc_ready, 1)
            t.wait_ge(peT_ready, 2)
            for q in range(2):
                for b in range(TB):
                    i = t.transpose(ps[:, 2, T * q + P * b:T * q + P * b + P],
                                    pc[:, b, 4 * q:4 * q + 4, :].rearrange("p h n -> p (h n)"), ident[:])
            i.then_inc(pcT_done, 1)
            t.wait_ge(pcT_ready, 1)
            t.wait_ge(gl_step, 2)

            def scores(u):
                kind, h = units[u]
                bank = ps[:, u % 2, :]
                if u >= 2:
                    t.wait_ge(exp_done, u - 1)
                if kind == "mem":
                    for b in range(TB):
                        i = mm(bank[:, T * b:T * b + T], qmT[:, h, P * b:P * b + P], kmT[:, h, :],
                               start=True, stop=True)
                    i.then_inc(score_done, 1)
                    return
                if kind == "fox":
                    t.wait_ge(cum_rows, 16 * FH)
                    q, k = qfk[:, 0, h, :], qfk[:, 1, h, :]
                else:
                    half = slice(HD * (h // REP), HD * (h // REP) + HD)
                    q, k = qT[half, h % REP, :], kT[half, 0 if kind == "slc" else 1, :]
                mm(bank[:, 0:P], q[:, 0:P], k[:, 0:P], start=True, stop=False)
                mm(bank[:, 0:P], identb[:], causal[:], start=False, stop=True)
                mm(bank[:, P:3 * P], q[:, P:T], k[:, :], start=True, stop=False)
                mm(bank[:, 2 * P:3 * P], identb[:], causal[:], start=False, stop=True).then_inc(score_done, 1)

            def transposed(u):
                t.wait_ge(prob_ready, u + 1)
                if u >= 2:
                    t.wait_ge(probT_ready, u - 1)
                n = 4 if units[u][0] == "mem" else 3
                src = (0, 2, 1, 3) if n == 4 else (0, 1, 2)
                for k in range(n):
                    i = t.transpose(ps[:, 2 + u % 2, P * k:P * k + P], prob[:, u % 2, P * src[k]:P * src[k] + P],
                                    ident[:])
                i.then_inc(probT_done, 1)

            def values(u):
                kind, h = units[u]
                t.wait_ge(probT_ready, u + 1)
                og = closed[min(c for c in closed if c >= u)]
                bank = ps[:, 4 + og % 2, :]
                pT = probT[:, u % 2, :]
                if og >= 2 and (u - 1) in closed:
                    t.wait_ge(heads_copied, og - 1)
                if kind == "mem":
                    mm(bank[:, 0:T], vm[:, 0, P * h:P * h + P], pT[:, 0:T], start=True, stop=False)
                    i = mm(bank[:, 0:T], vm[:, 1, P * h:P * h + P], pT[:, T:2 * T], start=False, stop=True)
                else:
                    rows = slice(HD * (h % 2), HD * (h % 2) + HD)
                    if kind == "fox":
                        v0, v1 = (vf[:, b, HD * h:HD * h + HD] for b in range(TB))
                    else:
                        g = h // REP
                        v0, v1 = (vsw[:, b, 0 if kind == "slc" else 1, HD * g:HD * g + HD] for b in range(TB))
                    if kind == "slc":
                        quarter = slice(32 * (h % 4), 32 * (h % 4) + NCMP)
                        mm(bank[rows, 0:T], vcmp[quarter, g, :], pcT[quarter, h // 4, :], start=True, stop=False)
                    mm(bank[rows, 0:T], v0, pT[:, 0:T], start=kind == "fox", stop=False)
                    i = mm(bank[rows, P:T], v1, pT[:, T:T + P], start=False, stop=kind != "slc")
                if u in closing:
                    i.then_inc(heads_done, 1)

            for s in range(len(units) + 1):
                if s < len(units):
                    scores(s)
                    filler()
                if s >= 1:
                    transposed(s - 1)
                if s < len(units):
                    filler()
                if s >= 1:
                    values(s - 1)

            t.wait_ge(heads_copied, len(closed))
            for m in range(fox0, fox0 + KC):
                branch_tile(m)
            def keep_warm(n):
                for _ in range(n):
                    mm(ps[:, 3, 0:T], ident[:], triU[:], start=True, stop=True)

            w_out_parts = [stream_parts(f"out{half}") for half in range(2)]
            for task in range(4):
                half, b = task // 2, task % 2
                for c in range(KC):
                    if b == 0 and c % 2 == 0:
                        t.wait_ge(w_low_ready, first_piece(at[f"out{half}"]) + c // 2 + 1)
                    if task == 0:
                        t.wait_ge(merged_low_ready, c // 2 + 1)
                    if task == 3 and c == 5:
                        t.wait_ge(x2_ready, 3)
                        rows_T(xs, 8, 4)
                        rows_T(xs, 9, 5)
                    i = split_mm(ps[:, 2 * b + half, :],
                                 [m[:, k, P * b:P * b + P] for m, k in ((merged_high[c // 4], c % 4), (mT_parts[1], c))],
                                 [m[:, c, :] for m in w_out_parts[half]], c == 0, c == KC - 1)
                i.then_inc(out_done, 1)
                if b == 1:
                    t.wait_ge(out_done, task + 1)
                    release()
            t.wait_ge(late_in, 32)
            for b in range(TB):
                if b == 1:
                    t.wait_ge(x2_ready, 4)
                    rows_T(xs, 10, 6)
                    rows_T(xs, 11, 7)
                t.wait_ge(hT_ready, 10 + 2 * b)
                for c in range(KC):
                    i = mm(ps[:, 0, NE * b:NE * b + NE], hT[:, c, P * b:P * b + P], wrout[:, c, :],
                           start=c == 0, stop=c == KC - 1)
            i.then_inc(router_done, 1)
            keep_warm(7)
            t.wait_ge(sel_table, 1)
            mm(ps[:, 1, 0:NE], triU[:, 0:P], sel[:, 0, :], start=True, stop=True)
            mm(ps[:, 1, NE:2 * NE], triU[:, P:T], sel[:, 0, :], start=True, stop=False)
            mm(ps[:, 1, NE:2 * NE], triU[:, 0:P], sel[:, 1, :], start=False, stop=True)
            mm(ps[:, 1, 2 * NE:3 * NE], triU[:, P:T], sel[:, 0, :], start=True, stop=False)
            mm(ps[:, 1, 2 * NE:3 * NE], triU[:, P:T], sel[:, 1, :], start=False, stop=True).then_inc(pos_done, 1)
            keep_warm(6)
            t.wait_ge(tables_ready, 1)
            most = t.value_load(cnti[0:1, 0:1], min_val=0, max_val=T)

            xview = xn[:, :, :].rearrange("p b (k c) -> p b c k", c=KC)

            def gather(g):
                t.wait_ge(sel_ready, g + 1)
                for c in range(KC):
                    for b in range(TB):
                        i = mm(ps[:, 2, CAP * c:CAP * c + CAP], xview[:, b, c, :], S[:, b, :],
                               start=b == 0, stop=b == TB - 1)
                i.then_inc(gather_done, 1)

            def scatter(b, bank=6):
                for h in range(2):
                    half = slice(64 * h, 64 * h + 64)
                    i = mm(ps[:, bank + h, :], ST[half, b, :], oE[half, :], start=True, stop=True)
                i.then_inc(scatter_done, 1)

            def item(level, e, first, places=places_of_all):
                n, g = NE * level + e, (NE + 1) * level + e
                t.wait_ge(ohg_ready, g + 1)
                t.wait_ge(xt_ready, g + 1)
                for k in range(2):
                    for h in range(2):
                        half = slice(64 * h, 64 * h + 64)
                        mm(ps[half, k, :], oneh[:, 0, :], biases[:, F * h + 512 * k:F * h + 512 * k + 512],
                           start=True, stop=False)
                for c in range(KC):
                    t.wait_ge(slot_full[c], 16 * (n + 1))
                    for k in range(2):
                        for h in range(2):
                            half = slice(64 * h, 64 * h + 64)
                            i = mm(ps[half, k, :], xT[:, c, :], places[c][:, F * h + 512 * k:F * h + 512 * k + 512],
                                   start=False, stop=c == KC - 1)
                    i.then_inc(ring_used, 1)
                    if not first and c == 1:
                        t.wait_ge(out_copied, n)
                        t.wait_ge(st_copied, n)
                        scatter(0)
                    if not first and c == 4:
                        t.wait_ge(added, 2 * n - 1)
                        scatter(1)
                gather(g + 1)
                t.wait_ge(sg_ready, n + 1)
                for b in range(TB):
                    i = t.transpose(ps[:, 4, P * b:P * b + P], SG[:, b, :], ident[:])
                i.then_inc(st_done, 1)
                t.wait_ge(act_ready, n + 1)
                view = act.rearrange("p (m r) -> p r m", r=4)
                for r in range(4):
                    i = t.transpose(ps[:, 3, P * r:P * r + P], view[:, r, :], ident[:])
                i.then_inc(actT_done, 1)
                t.wait_ge(ohd_ready, n + 1)
                for h in range(2):
                    half = slice(64 * h, 64 * h + 64)
                    mm(ps[half, 5, :], oneh[:, 1, :], biases[:, 2 * F + 512 * h:2 * F + 512 * h + 512],
                       start=True, stop=False)
                t.wait_ge(actT_copied, n + 1)
                for s in range(4):
                    t.wait_ge(slot_full[KC + s], 16 * (n + 1))
                    for k in range(2):
                        r = 2 * (s % 2) + k
                        lhs = actT[:, P * r + 64 * (s // 2):P * r + 64 * (s // 2) + 64]
                        for h in range(2):
                            half = slice(64 * h, 64 * h + 64)
                            i = mm(ps[half, 5, :], lhs, places[KC + s][:, 1024 * k + 512 * h:1024 * k + 512 * h + 512],
                                   start=False, stop=s == 3 and k == 1)
                    i.then_inc(ring_used, 1)

            def experts(level):
                if not isinstance(level, int):
                    t.wait_ge(xt_ready, (NE + 1) * level)
                gather((NE + 1) * level)
                if isinstance(level, int):
                    keep_warm(3)
                    item(level, 0, True, first_places)
                    item(level, 1, False, second_places)
                    item(level, 2, False, third_places)
                else:
                    item(level, 0, True)
                with t.Fori(3 if isinstance(level, int) else 1, NE) as e:
                    item(level, e, False)
                last = NE * level + NE - 1
                t.wait_ge(out_copied, last + 1)
                t.wait_ge(st_copied, last + 1)
                scatter(0)
                scatter(1, 0)
                t.wait_ge(added, 2 * last + 2)

            t.wait_ge(biases_in, 32)
            experts(0)
            with t.If(most > CAP):
                with t.Fori(1, LEVELS) as level:
                    experts(level)
            t.wait_ge(final_step, 1)


_INS = ['x', 'mem', 'g_mix', 'w_in', 'b_forget', 'b_merge', 'nsa_pe_k', 'nsa_w1_k', 'nsa_w2_k', 'nsa_pe_v',
        'nsa_w1_v', 'nsa_w2_v', 'g_mem', 'w_mem_kv', 'w_branch_nsa', 'w_branch_fox', 'w_branch_mem', 'w_out',
        'g_ffn', 'w_router', 'b_router', 'w_gate_up', 'b_gate_up', 'w_down', 'b_down', 'g_final']


def _rope_table(np, seq, dim):
    inv = (10000.0 ** (-np.arange(0, dim, 2, dtype=np.float32) / np.float32(dim))).astype(np.float32)
    ang = np.arange(seq, dtype=np.float32)[:, None] * inv[None, :]
    c, s = np.cos(ang), np.sin(ang)
    return np.concatenate([c, c, -s, s], axis=1).astype(np.float32)


def kernel(**inputs):
    import concourse.bacc as _bacc
    import numpy as np
    from concourse.bass_utils import run_bass_kernel_spmd as _run

    arrays = {"in_rope": _rope_table(np, 256, 64)}
    for name in _INS:
        arrays[f"in_{name}"] = np.ascontiguousarray(inputs[name])
    nc = _bacc.Bacc("TRN2", target_bir_lowering=False, num_devices=1)
    args = [nc.dram_tensor(n, a.shape, F32, kind="ExternalInput").ap() for n, a in arrays.items()]
    out = nc.dram_tensor("out_0", arrays["in_x"].shape, F32, kind="ExternalOutput").ap()
    hybrid_layer(nc, *args, out)
    r = _run(nc, [arrays], core_ids=[0])
    return r.results[0]["out_0"]
```
